# Optimizing a Trainium2 kernel written in Bass

```python
import math
import jax
import jax.numpy as jnp
from jax import lax
import numpy as np

D_MODEL = 1024
BATCH = 1
SEQ = 256
DEPTH = 2

GRID_W = 64
CTX_LEN = 256
HEAD_DIM = 64
BLOCK = 128
WINDOW = 128
ROPE_THETA = 10000.0
EPS = 1e-6
NEG_INF = -1e30
N_MOD = 6

MIX_WIDTH = D_MODEL
GROUP_WIDTH = MIX_WIDTH // 4
N_OUT_HEADS = MIX_WIDTH // HEAD_DIM
DIFF_HEADS = GROUP_WIDTH // HEAD_DIM
DIFF_QK_DIM = HEAD_DIM // 2
WIN_HEADS = GROUP_WIDTH // HEAD_DIM
WIN_KV_HEADS = WIN_HEADS // 2
GLOB_HEADS = GROUP_WIDTH // HEAD_DIM
GLOB_KV_HEADS = GLOB_HEADS // 2
HY_CH = GROUP_WIDTH
HY_ORDER = 2
HY_SHORT = 3
HY_BANDS = 16
HY_EMB = 1 + 2 * HY_BANDS
HY_HIDDEN = 64
HY_TARGET = 1e-2
HY_FAST = 0.3
HY_SLOW = 1.5

W_DIFF = 3 * DIFF_HEADS * HEAD_DIM
W_WIN = (WIN_HEADS + 2 * WIN_KV_HEADS) * HEAD_DIM
W_GLOB = (GLOB_HEADS + 2 * GLOB_KV_HEADS) * HEAD_DIM
W_HY = (HY_ORDER + 1) * HY_CH
D_IN = W_DIFF + W_WIN + W_GLOB + W_HY
SPLITS = (W_DIFF, W_DIFF + W_WIN, W_DIFF + W_WIN + W_GLOB)

PEER_HEADS = 8
N_KEYS = 128
N_EXPERTS = N_KEYS * N_KEYS
PEER_TOPK = 16
PEER_DK = 256
PEER_CHUNK = 128

kernel_name = 'hybrid_flow_backbone_peer'

def rmsnorm(x, g):
    xf = x.astype(jnp.float32)
    y = xf * lax.rsqrt(jnp.mean(xf * xf, axis=-1, keepdims=True) + EPS)
    return (y * g).astype(x.dtype)

def modulate(h, shift, scale):
    return h * (1.0 + scale) + shift

def axial_rope(n_tok, dim):
    rows = n_tok // GRID_W
    row = jnp.repeat(jnp.arange(rows, dtype=jnp.float32), GRID_W)
    col = jnp.tile(jnp.arange(GRID_W, dtype=jnp.float32), rows)
    axis_dim = dim // 2
    inv_freq = ROPE_THETA ** (-jnp.arange(0, axis_dim, 2, dtype=jnp.float32) / axis_dim)
    ang = jnp.concatenate([row[:, None] * inv_freq, col[:, None] * inv_freq], axis=-1)
    return jnp.cos(ang), jnp.sin(ang)

def apply_rope(x, cos, sin):
    shape = (1, x.shape[1]) + (1,) * (x.ndim - 3) + (cos.shape[-1],)
    c, s = cos.reshape(shape), sin.reshape(shape)
    x1, x2 = jnp.split(x.astype(jnp.float32), 2, axis=-1)
    return jnp.concatenate([x1 * c - x2 * s, x1 * s + x2 * c], axis=-1).astype(x.dtype)

def sink_softmax(s, sink):
    sink = sink.astype(jnp.float32)
    m = jnp.maximum(jnp.max(s, axis=-1, keepdims=True), sink)
    e = jnp.exp(s - m)
    return e / (jnp.sum(e, axis=-1, keepdims=True) + jnp.exp(sink - m))

def dense_attention(qs, ks, coefs, v, sink=None):
    B_, Lq, H, d = qs[0].shape
    G = v.shape[2]
    R = H // G
    dv = v.shape[-1]
    nb = Lq // BLOCK
    scale = d ** -0.5
    qb = tuple(q.reshape(B_, nb, BLOCK, G, R, d).swapaxes(0, 1) for q in qs)
    sink_b = None if sink is None else sink.reshape(1, G, R, 1, 1)

    def one_block(qblk):
        acc = None
        for q_, k_, coef in zip(qblk, ks, coefs):
            s = jnp.einsum('bqgrd,bkgd->bgrqk', q_, k_, preferred_element_type=jnp.float32) * scale
            p = jax.nn.softmax(s, axis=-1) if sink_b is None else sink_softmax(s, sink_b)
            acc = coef * p if acc is None else acc + coef * p
        return jnp.einsum('bgrqk,bkgd->bqgrd', acc.astype(v.dtype), v)

    o = lax.map(one_block, qb)
    return o.swapaxes(0, 1).reshape(B_, Lq, H, dv)

def window_attention(q, k, v, kc, vc, sink):
    B_, L_, H, d = q.shape
    G = k.shape[2]
    R = H // G
    nb = L_ // BLOCK
    scale = d ** -0.5

    def band(t):
        tb = t.reshape(B_, nb, BLOCK, G, t.shape[-1])
        pad = jnp.zeros_like(tb[:, :1])
        prev = jnp.concatenate([pad, tb[:, :-1]], axis=1)
        nxt = jnp.concatenate([tb[:, 1:], pad], axis=1)
        return jnp.concatenate([prev, tb, nxt], axis=2)

    kb, vb = band(k), band(v)
    qb = q.reshape(B_, nb, BLOCK, G, R, d)
    s_loc = jnp.einsum('bnqgrd,bnkgd->bgrnqk', qb, kb, preferred_element_type=jnp.float32) * scale
    qi = jnp.arange(BLOCK)[:, None]
    kj = jnp.arange(3 * BLOCK)[None, :]
    kpos = (jnp.arange(nb)[:, None, None] - 1) * BLOCK + kj
    valid = (jnp.abs(kj - BLOCK - qi) <= WINDOW) & (kpos >= 0) & (kpos < L_)
    s_loc = jnp.where(valid, s_loc, NEG_INF)
    s_ctx = jnp.einsum('bnqgrd,bkgd->bgrnqk', qb, kc, preferred_element_type=jnp.float32) * scale
    p = sink_softmax(jnp.concatenate([s_ctx, s_loc], axis=-1), sink.reshape(1, G, R, 1, 1, 1))
    p = p.astype(v.dtype)
    n_ctx = kc.shape[1]
    o = (jnp.einsum('bgrnqk,bkgd->bnqgrd', p[..., :n_ctx], vc)
         + jnp.einsum('bgrnqk,bnkgd->bnqgrd', p[..., n_ctx:], vb))
    return o.reshape(B_, L_, H, d)

def gqa_heads(t, n_q, n_kv, g_qk):
    B_, L_, _ = t.shape
    q, k, v = jnp.split(t, [n_q * HEAD_DIM, (n_q + n_kv) * HEAD_DIM], axis=-1)
    q = rmsnorm(q.reshape(B_, L_, n_q, HEAD_DIM), g_qk[0])
    k = rmsnorm(k.reshape(B_, L_, n_kv, HEAD_DIM), g_qk[1])
    return q, k, v.reshape(B_, L_, n_kv, HEAD_DIM)

def diff_attention(p, pc, g_qk, lam_vec, lambda_init, rope, want_ctx):
    def heads(t):
        B_, L_, _ = t.shape
        q, k, v = jnp.split(t, 3, axis=-1)
        q = rmsnorm(q.reshape(B_, L_, DIFF_HEADS, 2, DIFF_QK_DIM), g_qk[0])
        k = rmsnorm(k.reshape(B_, L_, DIFF_HEADS, 2, DIFF_QK_DIM), g_qk[1])
        return q, k, v.reshape(B_, L_, DIFF_HEADS, HEAD_DIM)

    q, k, v = heads(p)
    qc, kc, vc = heads(pc)
    q, k = apply_rope(q, *rope), apply_rope(k, *rope)
    lam_vec = lam_vec.astype(jnp.float32)
    lam = jnp.exp(jnp.sum(lam_vec[0] * lam_vec[1])) - jnp.exp(jnp.sum(lam_vec[2] * lam_vec[3])) + lambda_init
    coefs = (1.0, -lam)
    kk = jnp.concatenate([kc, k], axis=1)
    vv = jnp.concatenate([vc, v], axis=1)
    o = dense_attention((q[..., 0, :], q[..., 1, :]), (kk[..., 0, :], kk[..., 1, :]), coefs, vv)
    if not want_ctx:
        return o, None
    oc = dense_attention((qc[..., 0, :], qc[..., 1, :]), (kc[..., 0, :], kc[..., 1, :]), coefs, vc)
    return o, oc

def short_conv(u, w, b):
    up = jnp.pad(u, ((0, 0), (1, 1), (0, 0)))
    return up[:, :-2] * w[0] + up[:, 1:-1] * w[1] + up[:, 2:] * w[2] + b

def hyena_filters(n_tok, w1, b1, w2, b2, w3, b3, freq):
    t = jnp.linspace(0.0, 1.0, n_tok, dtype=jnp.float32)[:, None]
    w = (2.0 * math.pi / n_tok) * jnp.arange(n_tok, dtype=jnp.float32)[:, None]
    f = jnp.linspace(1e-4, HY_BANDS - 1, HY_BANDS, dtype=jnp.float32)[None, :]
    feat = jnp.concatenate([t, jnp.cos(f * w), -jnp.sin(f * w)], axis=-1)
    hdn = jnp.sin(freq * (feat @ w1 + b1))
    hdn = jnp.sin(freq * (hdn @ w2 + b2))
    filt = (hdn @ w3 + b3).astype(jnp.float32).reshape(n_tok, HY_ORDER, 2, HY_CH)
    deltas = jnp.abs(jnp.linspace(math.log(HY_TARGET) / HY_SLOW, math.log(HY_TARGET) / HY_FAST, HY_CH,
                                  dtype=jnp.float32))
    filt = filt * jnp.exp(-t[:, :, None, None] * deltas)
    fwd, bwd = filt[:, :, 0], filt[:, :, 1]
    kfull = jnp.concatenate([fwd, jnp.zeros_like(fwd[:1]), bwd[1:][::-1]], axis=0)
    return kfull / jnp.sum(jnp.abs(kfull), axis=0, keepdims=True)

def long_conv(z, kf):
    n = z.shape[1]
    zf = jnp.fft.rfft(z.astype(jnp.float32), n=2 * n, axis=1)
    hf = jnp.fft.rfft(kf, n=2 * n, axis=0)
    return jnp.fft.irfft(zf * hf[None], n=2 * n, axis=1)[:, :n].astype(z.dtype)

def hyena(u, conv_w, conv_b, filter_params, bias):
    n = u.shape[1]
    u = short_conv(u, conv_w, conv_b)
    v, x1, x2 = jnp.split(u, 3, axis=-1)
    kfull = hyena_filters(n, *filter_params)
    z = x1 * (long_conv(v, kfull[:, 0]) + bias[0] * v)
    return x2 * (long_conv(z, kfull[:, 1]) + bias[1] * z)

def merge_heads(o, g, w_out, lambda_init):
    B_, L_, _ = o.shape
    oh = rmsnorm(o.reshape(B_, L_, N_OUT_HEADS, HEAD_DIM), g.reshape(N_OUT_HEADS, HEAD_DIM))
    head_scale = jnp.where(jnp.arange(N_OUT_HEADS) < DIFF_HEADS, 1.0 - lambda_init, 1.0)[:, None]
    return (oh * head_scale.astype(oh.dtype)).reshape(B_, L_, MIX_WIDTH) @ w_out

def flat_heads(o):
    return o.reshape(o.shape[0], o.shape[1], -1)

def token_mixing(h, hc, rope_half, rope_full, lambda_init, want_ctx, w_in, g_qk_diff, lambda_diff,
                 g_qk_win, sink_win, g_qk_glob, hy_conv_w, hy_conv_b, hy_filter_params, hy_bias,
                 g_mix_out, w_out):
    pa, pw, pg, ph = jnp.split(h @ w_in, SPLITS, axis=-1)
    pac, pwc, pgc, phc = jnp.split(hc @ w_in, SPLITS, axis=-1)
    oa, oac = diff_attention(pa, pac, g_qk_diff, lambda_diff, lambda_init, rope_half, want_ctx)
    qw, kw, vw = gqa_heads(pw, WIN_HEADS, WIN_KV_HEADS, g_qk_win)
    qwc, kwc, vwc = gqa_heads(pwc, WIN_HEADS, WIN_KV_HEADS, g_qk_win)
    qw, kw = apply_rope(qw, *rope_full), apply_rope(kw, *rope_full)
    ob = window_attention(qw, kw, vw, kwc, vwc, sink_win)
    qg, kg, vg = gqa_heads(pg, GLOB_HEADS, GLOB_KV_HEADS, g_qk_glob)
    qgc, kgc, vgc = gqa_heads(pgc, GLOB_HEADS, GLOB_KV_HEADS, g_qk_glob)
    qg, kg = apply_rope(qg, *rope_full), apply_rope(kg, *rope_full)
    og = dense_attention((qg,), (jnp.concatenate([kgc, kg], axis=1),), (1.0,),
                         jnp.concatenate([vgc, vg], axis=1))
    oh = hyena(ph, hy_conv_w, hy_conv_b, hy_filter_params, hy_bias)
    lat = merge_heads(jnp.concatenate([flat_heads(oa), flat_heads(ob), flat_heads(og), oh], axis=-1),
                      g_mix_out, w_out, lambda_init)
    if not want_ctx:
        return lat, None
    obc = dense_attention((qwc,), (kwc,), (1.0,), vwc, sink=sink_win)
    ogc = dense_attention((qgc,), (kgc,), (1.0,), vgc)
    ohc = hyena(phc, hy_conv_w, hy_conv_b, hy_filter_params, hy_bias)
    ctx_out = merge_heads(jnp.concatenate([flat_heads(oac), flat_heads(obc), flat_heads(ogc), ohc], axis=-1),
                          g_mix_out, w_out, lambda_init)
    return lat, ctx_out

def peer(h, wq, keys, u_tab, v_tab):
    B_, L_, D_ = h.shape
    T = B_ * L_
    xt = h.reshape(T, D_)
    q = (xt @ wq).reshape(T, PEER_HEADS, 2, PEER_DK // 2)
    s = jnp.einsum('thpd,hpkd->thpk', q, keys, preferred_element_type=jnp.float32)
    s_top, i_top = lax.top_k(s, PEER_TOPK)
    cand = (s_top[..., 0, :, None] + s_top[..., 1, None, :]).reshape(T, PEER_HEADS, PEER_TOPK * PEER_TOPK)
    cidx = (i_top[..., 0, :, None] * N_KEYS + i_top[..., 1, None, :]).reshape(T, PEER_HEADS, PEER_TOPK * PEER_TOPK)
    best, pos = lax.top_k(cand, PEER_TOPK)
    experts = jnp.take_along_axis(cidx, pos, axis=-1)
    gate = jax.nn.softmax(best, axis=-1).astype(h.dtype)
    nc = T // PEER_CHUNK

    def one_chunk(args):
        xch, ech, gch = args
        act = jax.nn.gelu(jnp.einsum('chkd,cd->chk', u_tab[ech], xch))
        return jnp.einsum('chk,chkd->cd', gch * act, v_tab[ech])

    out = lax.map(one_chunk, (xt.reshape(nc, PEER_CHUNK, D_),
                              experts.reshape(nc, PEER_CHUNK, PEER_HEADS, PEER_TOPK),
                              gate.reshape(nc, PEER_CHUNK, PEER_HEADS, PEER_TOPK)))
    return out.reshape(B_, L_, D_)

def setup_inputs(seed: int = 0) -> dict:
    key = jax.random.key(seed)
    ks = iter(jax.random.split(key, 40))

    def nrm(shape, s):
        return jax.random.normal(next(ks), shape, jnp.float32) * s

    def gain(shape):
        return 1.0 + nrm(shape, 0.02)

    Ld = DEPTH
    return {
        'x': nrm((BATCH, SEQ, D_MODEL), 1.0),
        'c': nrm((BATCH, D_MODEL), 1.0),
        'ctx': nrm((BATCH, CTX_LEN, D_MODEL), 1.0),
        'c_ctx': nrm((D_MODEL,), 1.0),
        'w_mod': nrm((Ld, D_MODEL, N_MOD * D_MODEL), 0.5 * D_MODEL ** -0.5),
        'b_mod': nrm((Ld, N_MOD * D_MODEL), 0.01),
        'g_norm_mix': gain((Ld, D_MODEL)),
        'w_in': nrm((Ld, D_MODEL, D_IN), D_MODEL ** -0.5),
        'g_qk_diff': gain((Ld, 2, DIFF_QK_DIM)),
        'lambda_diff': nrm((Ld, 4, DIFF_QK_DIM), 0.1),
        'g_qk_win': gain((Ld, 2, HEAD_DIM)),
        'sink_win': nrm((Ld, WIN_HEADS), 0.5),
        'g_qk_glob': gain((Ld, 2, HEAD_DIM)),
        'hy_conv_w': nrm((Ld, HY_SHORT, W_HY), 0.5),
        'hy_conv_b': nrm((Ld, W_HY), 0.02),
        'hy_w1': nrm((Ld, HY_EMB, HY_HIDDEN), HY_EMB ** -0.5),
        'hy_b1': nrm((Ld, HY_HIDDEN), 0.1),
        'hy_w2': nrm((Ld, HY_HIDDEN, HY_HIDDEN), HY_HIDDEN ** -0.5),
        'hy_b2': nrm((Ld, HY_HIDDEN), 0.1),
        'hy_w3': nrm((Ld, HY_HIDDEN, 2 * HY_ORDER * HY_CH), HY_HIDDEN ** -0.5),
        'hy_b3': nrm((Ld, 2 * HY_ORDER * HY_CH), 0.02),
        'hy_freq': 1.0 + nrm((Ld, HY_HIDDEN), 0.1),
        'hy_bias': nrm((Ld, HY_ORDER, HY_CH), 0.5),
        'g_mix_out': gain((Ld, MIX_WIDTH)),
        'w_out': nrm((Ld, MIX_WIDTH, D_MODEL), MIX_WIDTH ** -0.5),
        'g_norm_ffn': gain((Ld, D_MODEL)),
        'peer_wq': nrm((Ld, D_MODEL, PEER_HEADS * PEER_DK), D_MODEL ** -0.5),
        'peer_keys': nrm((Ld, PEER_HEADS, 2, N_KEYS, PEER_DK // 2), (PEER_DK // 2) ** -0.5),
        'peer_u': nrm((Ld, N_EXPERTS, D_MODEL), D_MODEL ** -0.5),
        'peer_v': nrm((Ld, N_EXPERTS, D_MODEL), PEER_HEADS ** -0.5),
    }

def reference(x, c, ctx, c_ctx, w_mod, b_mod, g_norm_mix, w_in, g_qk_diff, lambda_diff, g_qk_win,
              sink_win, g_qk_glob, hy_conv_w, hy_conv_b, hy_w1, hy_b1, hy_w2, hy_b2, hy_w3, hy_b3,
              hy_freq, hy_bias, g_mix_out, w_out, g_norm_ffn, peer_wq, peer_keys, peer_u, peer_v):
    n_tok = x.shape[1]
    rope_half = axial_rope(n_tok, DIFF_QK_DIM)
    rope_full = axial_rope(n_tok, HEAD_DIM)
    xc = ctx
    sc = jax.nn.silu(c)
    scc = jax.nn.silu(c_ctx)
    for i in range(DEPTH):
        want_ctx = i < DEPTH - 1
        lambda_init = 0.8 - 0.6 * math.exp(-0.3 * i)
        m = (sc @ w_mod[i] + b_mod[i])[:, None, :]
        mc = scc @ w_mod[i] + b_mod[i]
        sh1, s1, g1, sh2, s2, g2 = jnp.split(m, N_MOD, axis=-1)
        sh1c, s1c, g1c, sh2c, s2c, g2c = jnp.split(mc, N_MOD, axis=-1)
        h = modulate(rmsnorm(x, g_norm_mix[i]), sh1, s1)
        hc = modulate(rmsnorm(xc, g_norm_mix[i]), sh1c, s1c)
        filt = (hy_w1[i], hy_b1[i], hy_w2[i], hy_b2[i], hy_w3[i], hy_b3[i], hy_freq[i])
        o, oc = token_mixing(h, hc, rope_half, rope_full, lambda_init, want_ctx, w_in[i], g_qk_diff[i],
                             lambda_diff[i], g_qk_win[i], sink_win[i], g_qk_glob[i], hy_conv_w[i],
                             hy_conv_b[i], filt, hy_bias[i], g_mix_out[i], w_out[i])
        x = x + g1 * o
        h2 = modulate(rmsnorm(x, g_norm_ffn[i]), sh2, s2)
        x = x + g2 * peer(h2, peer_wq[i], peer_keys[i], peer_u[i], peer_v[i])
        if want_ctx:
            xc = xc + g1c * oc
            h2c = modulate(rmsnorm(xc, g_norm_ffn[i]), sh2c, s2c)
            xc = xc + g2c * peer(h2c, peer_wq[i], peer_keys[i], peer_u[i], peer_v[i])
    return x


_drawn_inputs = setup_inputs


def setup_inputs(seed=0):
    import zlib

    import numpy as np

    out = dict(_drawn_inputs(seed))
    spreads = {}
    factors = {'g_norm_mix': 4.752,
     'g_qk_diff': 8.0,
     'lambda_diff': 5.602,
     'g_qk_win': 8.0,
     'sink_win': 8.0,
     'g_qk_glob': 8.0,
     'hy_conv_b': 4.398,
     'hy_b3': 6.177,
     'hy_freq': 4.1,
     'g_mix_out': 5.162,
     'g_norm_ffn': 4.665}
    for name, (base, spread) in spreads.items():
        noise = np.random.default_rng([zlib.crc32(name.encode()), seed]).standard_normal(out[name].shape)
        drawn = base * np.exp(spread * noise) if base else spread * noise
        out[name] = jnp.asarray(drawn.astype(out[name].dtype))
    for name, factor in factors.items():
        out[name] = (out[name] * factor).astype(out[name].dtype)
    return out
```

```python
import math
from contextlib import ExitStack

import concourse.bass as bass
import numpy as np
from concourse import mybir

F32 = mybir.dt.float32
U32 = mybir.dt.uint32
I32 = mybir.dt.int32
ALU = mybir.AluOpType
ACT = mybir.ActivationFunctionType
X = mybir.AxisListType.X

P = 128
D = 1024
KC = D // P
DEPTH = 2
SEQ = 256
TT = SEQ // P
HD = 64
EPS = 1e-6
CW = 256
N_MOD = 6
GRID_W = 64
BANDS = 16
CTX, LAT = 0, 1

DQ, WQ, GQ, DK, WGK, DV, WGV, HY0 = range(8)
N_IN = 10
QK_AT = {DQ: 0, DK: 256, WQ: 512, GQ: 768, WGK: 1024}
QK_W = 1280

HEADS = 8
N_KEYS = 128
N_EXPERTS = N_KEYS * N_KEYS
TOPK = 16
NE = HEADS * TOPK
STEP = 4
STEPS = NE // STEP
UR = VR = STEP
IXB = 4

C_BMOD, C_GMIX, C_GFFN, C_GOUT, C_CONVW, C_CONVB, C_HYB, N_COLS = 0, 48, 56, 64, 72, 90, 96, 100
R_GQK, R_SINK, R_LAM, N_ROWS = 0, QK_W, QK_W + 4, QK_W + 4 + 128
T_C32, T_S32, T_C64, T_S64, T_MASK, N_TAB = 0, 16, 32, 64, 96, 224
NFB = 5
SCR = 5120
BANKS = 5
MAGIC = 1.5 * 2.0 ** 23
GELU_C = 0.044715
GELU_S = math.sqrt(2.0 / math.pi)


class Signal:

    def __init__(self, sem, name, ledger, step=1):
        self.sem, self.step, self.n = sem, step, 0
        self.counts = ledger.setdefault(name, {})

    def mark(self, *event):
        self.n += self.step
        self.counts[event or (self.n,)] = self.n
        return self.sem, self.step

    def also(self, *event):
        self.counts[event] = self.n

    def at(self, *event):
        return self.sem, self.counts.get(event, 1)

    def knows(self, *event):
        return event in self.counts


def weight_order():
    order = []
    for l in range(DEPTH):
        order += [("mod", l, j) for j in range(N_MOD * D // CW)]
        for s in (CTX, LAT):
            full = s == LAT or l < DEPTH - 1
            order += [("in", l, j, s) for j in (range(N_IN) if full else (DK, WGK, DV, WGV))]
            if full:
                order += [("out", l, j, s) for j in range(D // CW)]
                order += [("wq", l, j, s) for j in range(HEADS)]
    return order


WS = 3


def product_of(kind, l, j, s=None):
    if kind == "mod":
        return ("mod", l, j // 2) if j % 2 else ("modhalf", l, j // 2)
    return {"in": "in", "out": "out", "wq": "pq"}[kind], l, s, j


def build(nc, dram, ledger):
    ctx = ExitStack()
    with ctx:
        def sb(name, shape, dt=F32):
            return ctx.enter_context(nc.sbuf_tensor(name, shape, dt))

        def signal(name, step=1):
            return Signal(ctx.enter_context(nc.semaphore(name)), name, ledger, step)

        xT = sb("xT", [P, KC, 2 * SEQ])
        hT = sb("hT", [P, KC, SEQ])
        ident = sb("ident", [P, P])
        ones = sb("ones", [P, P])
        zeros = sb("zeros", [P, P])
        half_ones = sb("half_ones", [P, P])
        norm_cols = sb("norm_cols", [P, 2])
        dft = sb("dft", [P, TT, 512])
        idft = sb("idft", [P, 4, SEQ])
        tab = sb("tab", [P, TT, N_TAB])
        cols = sb("cols", [P, DEPTH, N_COLS])
        rows = sb("rows", [P, N_ROWS])
        w_sb = sb("w_sb", [P, WS, KC, CW])
        cvec = sb("cvec", [P, 3, KC, 2])
        modrow = sb("modrow", [2, 2, 512])
        modT = sb("modT", [P, 48, 2])
        amix = sb("amix", [P, KC, 2])
        affn = sb("affn", [P, KC, 2])
        gout = sb("gout", [P, KC])
        lam = sb("lam", [P, 64 + 8])
        neglam = sb("neglam", [P, 1])
        negsink = sb("negsink", [P, 4])
        rstd = sb("rstd", [P, SEQ])
        spec = sb("spec", [P, NFB, 2, SEQ])
        rnorm = sb("rnorm", [P, 4])
        fw1 = sb("fw1", [2 * BANDS + 1, DEPTH, 64])
        fw2 = sb("fw2", [64, DEPTH, 64])
        fcol = sb("fcol", [64, DEPTH, 3])
        scratch = sb("scratch", [P, SCR])
        qT = sb("qT", [P, 6, SEQ])
        kT = sb("kT", [P, 4, 2 * SEQ])
        vtok = sb("vtok", [P, 2 * TT, 512])
        stat = sb("stat", [P, 56 + 24])
        prob = sb("prob", [P, 2, 2, 2 * SEQ])
        probT = sb("probT", [P, 2, 4, P])
        mx = sb("mx", [P, 2, 2])
        negm = sb("negm", [P, 2, 2])
        zsum = sb("zsum", [P, 8, 2])
        sinke = sb("sinke", [P, 2])
        rz = sb("rz", [P, 8, 2])
        mixT = sb("mixT", [P, KC, SEQ])
        upad = sb("upad", [P, 6, SEQ + 2])
        zy = sb("zy", [P, 1536])
        otok = zy[:, :].rearrange("p (t n) -> p t n", t=TT)
        zt = zy[:, 0:512].rearrange("p (t n) -> p t n", t=TT)
        yspec = zy[:, 512:1536].rearrange("p (t n) -> p t n", t=4)
        h2tok = sb("h2tok", [P, TT, D])
        top8 = sb("top8", [P, 4, TOPK])
        idx_a = sb("idx_a", [P, TT, 2, HEADS, TOPK], U32)
        best = sb("best", [P, TT, HEADS, TOPK])
        pos = sb("pos", [P, TT, HEADS, TOPK], U32)
        gz = sb("gz", [P, 2, HEADS])
        gate = sb("gate", [P, TT, NE])
        expert = sb("expert", [P, TT, NE], U32)
        ix = sb("ix", [P, IXB, STEP], U32)
        urow = sb("urow", [P, UR, D])
        vrow = sb("vrow", [P, VR, D])
        dots = sb("dots", [P, 2, STEP])
        poly = sb("poly", [P, 2, STEP])
        th = sb("th", [P, 2, STEP])
        wexp = sb("wexp", [P, 2, STEP])
        diag = sb("diag", [P, VR, P])
        iota16 = sb("iota16", [P, TOPK])

        ptok = scratch[:, 0:2 * QK_W].rearrange("p (t n) -> p t n", t=TT)
        qk_a = scratch[:, 2 * QK_W:3 * QK_W]
        qk_b = scratch[:, 3 * QK_W:4 * QK_W]
        osq = scratch[:, 2 * QK_W:2 * QK_W + TT * 768].rearrange("p (t h d) -> p t h d", t=TT, d=HD)
        uc = scratch[:, 0:1536].rearrange("p (c n) -> p c n", c=6)
        hy = scratch[:, 1536:1536 + 2048].rearrange("p (c n) -> p c n", c=8)
        sq = scratch[:, 2560:2560 + 2048]
        fdft = scratch[:, 0:4 * NFB * P].rearrange("p (k n) -> p k n", k=4)
        filt = mixT[:, :, :].rearrange("p k n -> p (k n)").rearrange("p (t o n) -> p t o n", t=TT, o=4)
        afilt = vtok[:, :, :].rearrange("p k n -> p (k n)").rearrange("p (t o n) -> p t o n", t=TT, o=4)
        decay = scratch[:, 2560:2560 + 512].rearrange("p (t n) -> p t n", t=TT)
        feat = scratch[0:2 * BANDS + 1, 3072:3072 + SEQ]
        fh = scratch[0:65, 3328:3328 + SEQ]
        fn = scratch[0:64, 3584:3584 + SEQ]
        fr = scratch[0:64, 3840:3840 + SEQ]
        fw3 = zy[0:65, 0:1024]
        hot = scratch[:, 0:2048]
        cand = scratch[:, 2048:2304]
        cand2 = scratch[:, 2304:2560]
        work = scratch[:, 4608:4608 + P]
        pq = scratch[:, 2560:3584].rearrange("p (a b n) -> p a b n", a=2, b=2)
        pij = scratch[:, 3584:3840].rearrange("p (a n) -> p a n", a=2).bitcast(U32)
        pijf = scratch[:, 3840:4096].rearrange("p (a n) -> p a n", a=2)
        idx_f = scratch[:, 4096:4352].rearrange("p (a h k) -> p a h k", a=2, h=HEADS)
        eij = scratch[:, 4352:4608].rearrange("p (a n) -> p a n", a=2)
        keys = mixT[:, :, :].rearrange("p k n -> p (k n)").rearrange("p (c n) -> p c n", c=16)
        yacc = scratch[:, 2560:2560 + D]

        banks = [ctx.enter_context(nc.psum_tensor(f"bank{i}", [P, 512], F32)) for i in range(BANKS)]
        obank = ctx.enter_context(nc.psum_tensor("obank", [P, 512], F32))
        acc = [ctx.enter_context(nc.psum_tensor(f"acc{i}", [P, 512], F32)) for i in range(2)]

        consts_in = signal("consts_in", 16)
        rows_in = signal("rows_in", 16)
        filt_in = signal("filt_in", 16)
        keys_in = signal("keys_in", 16)
        weights_in = [signal(f"weights_in{i}", 16) for i in range(WS)]
        full = signal("full")
        read_v = signal("read_v")
        read_s = signal("read_s")
        v_step = signal("v_step")
        s_step = signal("s_step")
        v_ready = signal("v_ready")
        s_ready = signal("s_ready")
        p_ready = signal("p_ready")
        u_in = [signal(f"u_in{i}", 16) for i in range(UR)]
        v_in = [signal(f"v_in{i}", 16) for i in range(VR)]
        ix_ready = signal("ix_ready")
        u_used = signal("u_used")
        row_free = signal("row_free")
        poly_ready = signal("poly_ready")
        th_ready = signal("th_ready")
        w_ready = signal("w_ready")
        diag_ready = signal("diag_ready")
        v_used = signal("v_used")
        out_done = signal("out_done", 16)
        gelu_step = signal("gelu_step")

        bank_order = ledger.setdefault("bank_order", [])
        taken = []

        index_of = {k: i for i, k in enumerate(bank_order)}

        def bank_of(*key):
            return banks[index_of.get(key, 0) % BANKS]

        def emptied(key):
            return next((x.at(*key) for x in (read_v, v_ready, read_s) if x.knows(*key)), read_s.at(*key))

        passes = [(l, s) for l in range(DEPTH) for s in (CTX, LAT)]

        def is_full(l, s):
            return s == LAT or l < DEPTH - 1

        peer_tiles = [(l, s, t) for l, s in passes if is_full(l, s) for t in range(TT)]
        U_0, DIAG_0, V_0 = STEP, 2 * STEP, IXB * STEP

        block = ctx.enter_context(nc.Block())

        @block.sync
        def _(sp):
            for name, dst in (("cvec", cvec[:, 1, :, :]), ("x", None), ("ident", ident[:, :]), ("half_ones", half_ones[:, :]),
                              ("norm_cols", norm_cols[:, :]), ("dft", dft[:, :, :]), ("idft", idft[:, :, :]),
                              ("tab", tab[:, :, :]), ("cols", cols[:, :, :]), ("fw1", fw1[:, :, :]),
                              ("fw2", fw2[:, :, :]), ("fcol", fcol[:, :, :]), ("iota16", iota16[:, :])):
                if name == "x":
                    sp.dma_start(xT[:, :, 0:SEQ], dram["ctx"]).then_inc(*consts_in.mark())
                    sp.dma_start(xT[:, :, SEQ:2 * SEQ], dram["x"]).then_inc(*consts_in.mark("all"))
                else:
                    sp.dma_start(dst, dram[name]).then_inc(*consts_in.mark("all"))

            def load_layer(l):
                if l:
                    sp.wait_ge(*v_ready.at("x_ffn", l - 1, LAT, TT - 1, KC - 1))
                sp.dma_start(rows[:, :], dram["rows"][l, :, :]).then_inc(*rows_in.mark(l))
                sp.dma_start(fdft, dram["fdft"]).then_inc(*filt_in.mark())
                sp.dma_start(decay, dram["decay"]).then_inc(*filt_in.mark())
                sp.dma_start(feat, dram["feat"]).then_inc(*filt_in.mark())
                sp.dma_start(fw3[:, :], dram["fw3"][l, :, :]).then_inc(*filt_in.mark(l))

            order = weight_order()
            for n, (kind, l, j, *s) in enumerate(order):
                if kind == "mod" and j == 0:
                    load_layer(l)
                if kind == "wq" and j == 2:
                    sp.wait_ge(*full.at("out", l, *s, D // CW - 1))
                    sp.dma_start(keys, dram["keys"][l, :, :, :]).then_inc(*keys_in.mark(l, *s))
                if n >= WS:
                    sp.wait_ge(*full.at(*product_of(*order[n - WS])))
                sp.dma_start(w_sb[:, n % WS, :, :], dram[kind][l, j, :, :, :]).then_inc(*weights_in[n % WS].mark(n))
            for c in range(KC):
                sp.wait_ge(*v_ready.at("x_ffn", DEPTH - 1, LAT, TT - 1, c))
                sp.dma_start(dram["y"][c * P:(c + 1) * P, :], xT[:, c, SEQ:2 * SEQ]).then_inc(*out_done.mark(c))
            sp.wait_ge(*out_done.at(KC - 1))

        @block.tensor
        def _(pe):
            mm = pe.matmul
            order = weight_order()
            used = [0]
            pe.sem_inc(v_used.sem, V_0)

            def take(*key):
                n = len(taken)
                if n >= BANKS:
                    pe.wait_ge(*emptied(taken[n - BANKS]))
                taken.append(key)
                return banks[n % BANKS]

            def weights(*what):
                n = used[0]
                assert order[n] == what, (order[n], what)
                used[0] += 1
                pe.wait_ge(*weights_in[n % WS].at(n))
                return w_sb[:, n % WS, :, :]

            def modulation(l):
                pe.wait_ge(*v_ready.at("silu"))
                pe.wait_ge(*consts_in.at("all"))

                def turn(n):
                    pe.wait_ge(*read_s.at("mod", l, n))
                    bank = take("modT", l, n)
                    for i in range(4):
                        ins = pe.transpose(bank[:, 2 * i:2 * i + 2], modrow[:, n % 2, i * P:(i + 1) * P], ident[0:2, 0:2])
                    ins.then_inc(*full.mark("modT", l, n))

                for n in range(12):
                    bank = take("mod", l, n)
                    for j in range(2):
                        w = weights("mod", l, 2 * n + j)
                        for k in range(KC):
                            ins = mm(bank[0:2, j * CW:(j + 1) * CW], cvec[:, 0, k, :], w[:, k, :],
                                     start=k == 0, stop=k == KC - 1)
                        ins.then_inc(*full.mark("mod" if j else "modhalf", l, n))
                    if n:
                        turn(n - 1)
                turn(11)

            def filters(l):
                pe.wait_ge(*filt_in.at(l))
                bank = take("fh1", l)
                mm(bank[0:64, 0:SEQ], fw1[:, l, :], feat, start=True, stop=True).then_inc(*full.mark("fh1", l))
                pe.wait_ge(*s_ready.at("fh1", l))
                bank = take("fh2", l)
                mm(bank[0:64, 0:SEQ], fw2[:, l, :], fh[0:64, :], start=True, stop=True).then_inc(*full.mark("fh2", l))
                pe.wait_ge(*s_ready.at("fh2", l))
                for t in range(TT):
                    for h in range(2):
                        bank = take("filt", l, t, h)
                        mm(bank[:, :], fh[:, t * P:(t + 1) * P], fw3[:, h * 512:(h + 1) * 512],
                           start=True, stop=True).then_inc(*full.mark("filt", l, t, h))
                pe.wait_ge(*read_v.at("filt", l, TT - 1, 1))
                for b in range(NFB):
                    bank = take("spec", l, b)
                    n = 0
                    for d in range(2):
                        for t in range(TT):
                            ins = mm(bank[:, :], fdft[:, d * TT + t, b * P:(b + 1) * P], filt[:, t, d:4:2, :],
                                     start=n == 0, stop=n == 3)
                            n += 1
                    ins.then_inc(*full.mark("spec", l, b))
                pe.wait_ge(*s_ready.at("afilt", l))
                bank = take("fnorm", l)
                for o in range(2):
                    for c in range(2):
                        n = 0
                        for d in range(2):
                            for t in range(TT):
                                ins = mm(bank[:, 2 * o + c:2 * o + c + 1], afilt[:, t, 2 * o + d, c * P:(c + 1) * P],
                                         norm_cols[:, int(d == 1 and t == 0):int(d == 1 and t == 0) + 1],
                                         start=n == 0, stop=n == 3)
                                n += 1
                ins.then_inc(*full.mark("fnorm", l))

            def norm(which, l, s):
                pe.wait_ge(*v_ready.at("sq", which, l, s))
                bank = take("norm", which, l, s)
                for k in range(KC):
                    ins = mm(bank[:, 0:SEQ], ones[:, :], sq[:, k * SEQ:(k + 1) * SEQ], start=k == 0, stop=k == KC - 1)
                ins.then_inc(*full.mark("norm", which, l, s))

            def in_proj(l, s):
                pe.wait_ge(*s_ready.at("h", "mix", l, s))
                for j in range(N_IN) if is_full(l, s) else (DK, WGK, DV, WGV):
                    w = weights("in", l, j, s)
                    bank = take("in", l, s, j)
                    for i in range(2):
                        for k in range(KC):
                            if j < HY0:
                                ins = mm(bank[:, i * CW:(i + 1) * CW], hT[:, k, i * P:(i + 1) * P], w[:, k, :],
                                         start=k == 0, stop=k == KC - 1)
                            else:
                                ins = mm(bank[:, i * CW:(i + 1) * CW], w[:, k, i * P:(i + 1) * P], hT[:, k, :],
                                         start=k == 0, stop=k == KC - 1)
                    ins.then_inc(*full.mark("in", l, s, j))

            def turn_qk(l, s):
                pe.wait_ge(*v_step.at("qk", l, s))
                groups = (0, 1), (2, 3), (4, 5, 6, 7), (8, 9)
                for t in range(TT):
                    for g, blocks in enumerate(groups):
                        if not is_full(l, s) and g in (0, 2):
                            continue
                        bank = take("qkT", l, s, t, g)
                        for i, b in enumerate(blocks):
                            ins = pe.transpose(bank[:, i * P:(i + 1) * P], ptok[:, t, b * P:(b + 1) * P], ident[:, :])
                        ins.then_inc(*full.mark("qkT", l, s, t, g))

            def attention(l, s):
                units = [(t, h) for t in range(TT) for h in range(12)]
                nk = SEQ if s == CTX else 2 * SEQ
                nb = nk // P
                pe.wait_ge(*read_s.at("qkT", l, s, TT - 1, 3))

                def scores(t, h):
                    for c in range(2 if h < 4 else 1):
                        bank = take("s", l, s, t, h, c)
                        if h < 4:
                            qb, kb, at, d = h // 2, h // 2, 64 * (h % 2) + 32 * c, 32
                        else:
                            qb, kb, at, d = 2 + 2 * (h // 4 - 1) + h % 2, 1 + h // 4, 64 * (h % 4 // 2), 64
                        mm(bank[:, 0:nk], qT[at:at + d, qb, t * P:(t + 1) * P], kT[at:at + d, kb, 0:nk],
                           start=True, stop=True).then_inc(*full.mark("s", l, s, t, h, c))

                def turn(t, h):
                    pe.wait_ge(*(v_ready.at("prob", l, s, t, h) if h < 4 else read_s.at("s", l, s, t, h, 0)))
                    bank = take("pT", l, s, t, h)
                    i = (t * 12 + h) % 2
                    for b in range(nb):
                        ins = pe.transpose(bank[:, b * P:(b + 1) * P], prob[:, i, 0, b * P:(b + 1) * P], ident[:, :])
                    ins.then_inc(*full.mark("pT", l, s, t, h))

                def values(t, h):
                    if h % 4 == 0 and (t, h) != (0, 0):
                        pe.wait_ge(*read_v.at("o", l, s, *units[t * 12 + h - 1]))
                    pe.wait_ge(*read_s.at("pT", l, s, t, h))
                    v = 64 * h if h < 4 else 256 + 128 * (h // 4 - 1) + 64 * (h % 4 // 2)
                    i = (t * 12 + h) % 2
                    for b in range(nb):
                        ins = mm(obank[:, 64 * (h % 4):64 * (h % 4) + 64], probT[:, i, b, :], vtok[:, b, v:v + 64],
                                 start=b == 0, stop=b == nb - 1)
                    ins.then_inc(*full.mark("o", l, s, t, h))

                n = len(units)
                for i in range(n + 2):
                    if i < n:
                        scores(*units[i])
                    if 1 <= i <= n:
                        turn(*units[i - 1])
                    if i >= 2:
                        values(*units[i - 2])

            def turn_o(l, s):
                pe.wait_ge(*v_ready.at("onorm", l, s))
                for t in range(TT):
                    for g in range(2):
                        bank = take("oT", l, s, t, g)
                        for i in range(3):
                            b = 3 * g + i
                            ins = pe.transpose(bank[:, i * P:(i + 1) * P], otok[:, t, b * P:(b + 1) * P], ident[:, :])
                        ins.then_inc(*full.mark("oT", l, s, t, g))

            def hyena(l, s):
                for o in range(2):
                    pe.wait_ge(*v_ready.at("z", l, s, o))
                    bank = take("zt", l, s, o)
                    for t in range(TT):
                        for c in range(2):
                            src = uc[:, c, t * P:(t + 1) * P] if o == 0 else hy[:, c, t * P:(t + 1) * P]
                            ins = pe.transpose(bank[:, t * CW + c * P:t * CW + (c + 1) * P], src, ident[:, :])
                    ins.then_inc(*full.mark("zt", l, s, o))
                    pe.wait_ge(*read_s.at("zt", l, s, o))
                    for r in range(2):
                        bank = take("zf", l, s, o, r)
                        for b in range(2):
                            for t in range(TT):
                                ins = mm(bank[:, b * CW:(b + 1) * CW], dft[:, t, (2 * r + b) * P:(2 * r + b + 1) * P],
                                         zt[:, t, :], start=t == 0, stop=t == TT - 1)
                        ins.then_inc(*full.mark("zf", l, s, o, r))
                    pe.wait_ge(*v_ready.at("yspec", l, s, o))
                    bank = take("y", l, s, o)
                    for c in range(2):
                        for b in range(4):
                            ins = mm(bank[:, c * SEQ:(c + 1) * SEQ], yspec[:, b, c * P:(c + 1) * P], idft[:, b, :],
                                     start=b == 0, stop=b == 3)
                    ins.then_inc(*full.mark("y", l, s, o))
                pe.wait_ge(*v_ready.at("hysq", l, s))
                bank = take("hynorm", l, s)
                for c in range(2):
                    ins = mm(bank[:, c * SEQ:(c + 1) * SEQ], half_ones[:, :], hy[:, 2 + c, :], start=True, stop=True)
                ins.then_inc(*full.mark("hynorm", l, s))

            def out_proj(l, s):
                pe.wait_ge(*read_s.at("oT", l, s, TT - 1, 1))
                pe.wait_ge(*v_ready.at("mixT", l, s))
                for j in range(D // CW):
                    w = weights("out", l, j, s)
                    bank = take("out", l, s, j)
                    for i in range(2):
                        for k in range(KC):
                            ins = mm(bank[:, i * SEQ:(i + 1) * SEQ], w[:, k, i * P:(i + 1) * P], mixT[:, k, :],
                                     start=k == 0, stop=k == KC - 1)
                    ins.then_inc(*full.mark("out", l, s, j))

            def peer_queries(l, s):
                pe.wait_ge(*s_ready.at("h", "ffn", l, s))
                for t in range(TT):
                    for g in range(2):
                        bank = take("h2", l, s, t, g)
                        for i in range(4):
                            ins = pe.transpose(bank[:, i * P:(i + 1) * P], hT[:, 4 * g + i, t * P:(t + 1) * P], ident[:, :])
                        ins.then_inc(*full.mark("h2", l, s, t, g))

                def key_scores(j):
                    pe.wait_ge(*read_s.at("pq", l, s, j))
                    bank = take("ks", l, s, j)
                    for t in range(TT):
                        for i in range(2):
                            ins = mm(bank[:, (2 * t + i) * P:(2 * t + i + 1) * P], pq[:, j % 2, i, t * P:(t + 1) * P],
                                     keys[:, 2 * j + i, :], start=True, stop=True)
                    ins.then_inc(*full.mark("ks", l, s, j))

                for j in range(HEADS):
                    w = weights("wq", l, j, s)
                    bank = take("pq", l, s, j)
                    for i in range(2):
                        for k in range(KC):
                            ins = mm(bank[:, i * SEQ:(i + 1) * SEQ], w[:, k, i * P:(i + 1) * P], hT[:, k, :],
                                     start=k == 0, stop=k == KC - 1)
                    ins.then_inc(*full.mark("pq", l, s, j))
                    if j == 0:
                        pe.wait_ge(*keys_in.at(l, s))
                    else:
                        key_scores(j - 1)
                key_scores(HEADS - 1)

            def experts(l, s, t):
                q = peer_tiles.index((l, s, t))
                if q:
                    pe.wait_ge(*s_ready.at("yacc", *peer_tiles[q - 1]))
                pe.wait_ge(*read_s.at("h2", l, s, TT - 1, 1))
                for a in range(2):
                    mm(acc[a][:, :], zeros[:, :], h2tok[:, t, 0:512], start=True, stop=False)
                with pe.Fori(q * STEPS, (q + 1) * STEPS) as i:
                    for j in range(STEP):
                        pe.wait_ge(v_in[j].sem, i * 16 + 16)
                        pe.wait_ge(diag_ready.sem, i * STEP + (j + 1 + DIAG_0))
                        mm(acc[0][:, :], diag[:, j, :], vrow[:, j, 0:512], start=False, stop=False)
                        mm(acc[1][:, :], diag[:, j, :], vrow[:, j, 512:D], start=False, stop=False).then_inc(v_used.sem, 1)
                for a in range(2):
                    ins = mm(acc[a][:, :], zeros[:, :], h2tok[:, t, 0:512], start=False, stop=True)
                ins.then_inc(*full.mark("acc", l, s, t))

            def turn_y(l, s, t):
                pe.wait_ge(*s_ready.at("yacc", l, s, t))
                for g in range(2):
                    bank = take("yT", l, s, t, g)
                    for i in range(4):
                        ins = pe.transpose(bank[:, i * P:(i + 1) * P], yacc[:, (4 * g + i) * P:(4 * g + i + 1) * P], ident[:, :])
                    ins.then_inc(*full.mark("yT", l, s, t, g))

            for l in range(DEPTH):
                modulation(l)
                filters(l)
                for s in (CTX, LAT):
                    norm("mix", l, s)
                    in_proj(l, s)
                    turn_qk(l, s)
                    if is_full(l, s):
                        attention(l, s)
                        turn_o(l, s)
                        hyena(l, s)
                        out_proj(l, s)
                        norm("ffn", l, s)
                        peer_queries(l, s)
                        for t in range(TT):
                            experts(l, s, t)
                            turn_y(l, s, t)

        @block.scalar
        def _(act):
            ac = nc.scalar.activation

            def done(ins, sig=s_step, *event):
                ins.then_inc(*sig.mark(*event))
                act.wait_ge(sig.sem, sig.n)

            act.sem_inc(diag_ready.sem, DIAG_0)
            act.wait_ge(*consts_in.at("all"))
            done(ac(cvec[:, 2, :, :], cvec[:, 1, :, :], ACT.Exp, scale=-1.0), s_ready, "exp_c")

            def modulation(l):
                for n in range(12):
                    act.wait_ge(*full.at("mod", l, n))
                    if n >= 2:
                        act.wait_ge(*full.at("modT", l, n - 2))
                    bank = bank_of("mod", l, n)
                    done(ac(modrow[:, n % 2, :], bank[0:2, :], ACT.Copy), read_s, "mod", l, n)

            def filters(l):
                act.wait_ge(*v_ready.at("lam", l))
                done(ac(lam[:, 66:68], lam[:, 64:66], ACT.Exp), s_ready, "lam", l)
                for n in (1, 2):
                    act.wait_ge(*v_ready.at(f"fr{n}", l))
                    done(ac(fh[0:64, :], fr, ACT.Sin), s_ready, f"fh{n}", l)
                act.wait_ge(*read_v.at("filt", l, TT - 1, 1))
                done(ac(afilt, filt, ACT.Abs), s_ready, "afilt", l)
                for b in range(NFB):
                    act.wait_ge(*full.at("spec", l, b))
                    done(ac(spec[:, b, :, :], bank_of("spec", l, b)[:, :].rearrange("p (o n) -> p o n", o=2), ACT.Copy),
                         read_s, "spec", l, b)

            def scaled(which, l, s):
                a, sh = (amix, 0) if which == "mix" else (affn, 24)
                act.wait_ge(*v_ready.at("xn", which, l, s))
                for k in range(KC):
                    ins = ac(hT[:, k, :], hT[:, k, :], ACT.Identity, bias=modT[:, sh + k, s:s + 1], scale=a[:, k, s:s + 1])
                    ins.then_inc(*(s_ready.mark("h", which, l, s) if k == KC - 1 else s_step.mark()))

            def in_proj(l, s):
                for j in range(N_IN) if is_full(l, s) else (DK, WGK, DV, WGV):
                    act.wait_ge(*full.at("in", l, s, j))
                    bank = bank_of("in", l, s, j)[:, :].rearrange("p (i n) -> p i n", i=2)
                    if j in QK_AT:
                        dst = ptok[:, :, QK_AT[j]:QK_AT[j] + CW]
                    elif j < HY0:
                        dst = vtok[:, 2 * s:2 * s + 2, (j - DV) * CW:(j - DV + 1) * CW]
                    else:
                        dst = upad[:, 2 * (j - HY0):2 * (j - HY0) + 2, 1:SEQ + 1]
                    done(ac(dst, bank, ACT.Copy), read_s, "in", l, s, j)

            def turn_qk(l, s):
                dests = (qT, 0), (kT, 0), (qT, 2), (kT, 2)
                for t in range(TT):
                    for g, (buf, at) in enumerate(dests):
                        if not is_full(l, s) and g in (0, 2):
                            continue
                        act.wait_ge(*full.at("qkT", l, s, t, g))
                        n = 4 if g == 2 else 2
                        off = t * P + (s * SEQ if buf is kT else 0)
                        bank = bank_of("qkT", l, s, t, g)[:, 0:n * P].rearrange("p (b n) -> p b n", b=n)
                        done(ac(buf[:, at:at + n, off:off + P], bank, ACT.Copy), read_s, "qkT", l, s, t, g)

            def attention(l, s):
                units = [(t, h) for t in range(TT) for h in range(12)]
                nk = SEQ if s == CTX else 2 * SEQ
                nb = nk // P

                def exps(t, h):
                    i = (t * 12 + h) % 2
                    z = (t * 12 + h) % 8
                    scale = (32 if h < 4 else 64) ** -0.5
                    for c in range(2 if h < 4 else 1):
                        act.wait_ge(*v_ready.at("negm", l, s, t, h, c))
                        if t * 12 + h >= 2:
                            act.wait_ge(*full.at("pT", l, s, *units[t * 12 + h - 2]))
                        bank = bank_of("s", l, s, t, h, c)
                        done(ac(prob[:, i, c, 0:nk], bank[:, 0:nk], ACT.Exp, bias=negm[:, i, c:c + 1], scale=scale,
                                accum_out=zsum[:, z, c:c + 1]), read_s, "s", l, s, t, h, c)
                    if 4 <= h < 8:
                        done(ac(sinke[:, i:i + 1], negsink[:, h - 4:h - 3], ACT.Exp, bias=negm[:, i, 0:1], scale=-1.0),
                             s_ready, "sinke", l, s, t, h)

                def turned(t, h):
                    i = (t * 12 + h) % 2
                    act.wait_ge(*full.at("pT", l, s, t, h))
                    if t * 12 + h >= 2:
                        act.wait_ge(*full.at("o", l, s, *units[t * 12 + h - 2]))
                    bank = bank_of("pT", l, s, t, h)[:, 0:nk].rearrange("p (b n) -> p b n", b=nb)
                    done(ac(probT[:, i, 0:nb, :], bank, ACT.Copy), read_s, "pT", l, s, t, h)

                for i in range(len(units) + 1):
                    if i < len(units):
                        exps(*units[i])
                    if i:
                        turned(*units[i - 1])

            def turn_o(l, s):
                for t in range(TT):
                    for g in range(2):
                        act.wait_ge(*full.at("oT", l, s, t, g))
                        for i in range(3):
                            b = 3 * g + i
                            done(ac(mixT[:, b, t * P:(t + 1) * P], bank_of("oT", l, s, t, g)[:, i * P:(i + 1) * P],
                                    ACT.Copy, scale=gout[:, b:b + 1]),
                                 *((read_s, "oT", l, s, t, g) if i == 2 else (s_step,)))

            def hyena(l, s):
                for o in range(2):
                    act.wait_ge(*full.at("zt", l, s, o))
                    done(ac(zt[:, :, :], bank_of("zt", l, s, o)[:, :].rearrange("p (t n) -> p t n", t=TT), ACT.Copy),
                         read_s, "zt", l, s, o)

            def peer_queries(l, s):
                for t in range(TT):
                    for g in range(2):
                        act.wait_ge(*full.at("h2", l, s, t, g))
                        done(ac(h2tok[:, t, g * 512:(g + 1) * 512], bank_of("h2", l, s, t, g)[:, :], ACT.Copy),
                             read_s, "h2", l, s, t, g)
                for j in range(HEADS):
                    act.wait_ge(*full.at("pq", l, s, j))
                    if j >= 2:
                        act.wait_ge(*full.at("ks", l, s, j - 2))
                    done(ac(pq[:, j % 2, :, :], bank_of("pq", l, s, j)[:, :].rearrange("p (i n) -> p i n", i=2),
                            ACT.Copy), read_s, "pq", l, s, j)
                for t in range(TT):
                    act.wait_ge(*v_ready.at("best", l, s, t))
                    done(ac(gate[:, t, :], gate[:, t, :], ACT.Exp), s_ready, "gate", l, s, t)

            def experts(l, s, t):
                q = peer_tiles.index((l, s, t))
                with act.Fori(q * STEPS // 2, (q + 1) * STEPS // 2) as i:
                    for g in range(2):
                        act.wait_ge(poly_ready.sem, i * 2 + (g + 1))
                        ac(th[:, g, :], poly[:, g, :], ACT.Tanh, scale=GELU_S).then_inc(th_ready.sem, 1)
                        act.wait_ge(w_ready.sem, i * 2 + (g + 1))
                        for j in range(STEP):
                            act.wait_ge(v_used.sem, i * 2 * STEP + (STEP * (g - 1) + j + 1 + V_0))
                            ac(diag[:, j, :], ident[:, :], ACT.Copy, scale=wexp[:, g, j:j + 1]).then_inc(diag_ready.sem, 1)
                act.wait_ge(*full.at("acc", l, s, t))
                for a in range(2):
                    done(ac(yacc[:, a * 512:(a + 1) * 512], acc[a][:, :], ACT.Copy),
                         *((s_ready, "yacc", l, s, t) if a else (s_step,)))

            for l in range(DEPTH):
                modulation(l)
                filters(l)
                for s in (CTX, LAT):
                    scaled("mix", l, s)
                    in_proj(l, s)
                    turn_qk(l, s)
                    if is_full(l, s):
                        attention(l, s)
                        turn_o(l, s)
                        hyena(l, s)
                        scaled("ffn", l, s)
                        peer_queries(l, s)
                        for t in range(TT):
                            experts(l, s, t)

        @block.vector
        def _(dve):
            v = nc.vector

            def done(ins, sig=v_step, *event):
                ins.then_inc(*sig.mark(*event))
                dve.wait_ge(sig.sem, sig.n)

            dve.sem_inc(u_used.sem, U_0)
            def root(x, n, y, t):
                done(v.tensor_scalar(x, x, EPS * n, None, ALU.add))
                done(v.tensor_scalar(y.bitcast(I32), x.bitcast(I32), -0.5, float(0x5F3759DF), ALU.mult, ALU.add))
                for k in range(3):
                    done(v.tensor_tensor(t, y, y, ALU.mult))
                    done(v.scalar_tensor_tensor(t, t, -0.5, x, ALU.mult, ALU.mult))
                    done(v.scalar_tensor_tensor(x if k == 2 else y, t, 1.5, y, ALU.add, ALU.mult))

            done(v.memset(ones[:, :], 1.0))
            done(v.memset(zeros[:, :], 0.0))
            done(v.memset(upad[:, :, :], 0.0))
            done(v.memset(sinke[:, :], 0.0))
            dve.wait_ge(*s_ready.at("exp_c"))
            done(v.tensor_scalar(cvec[:, 2, :, :], cvec[:, 2, :, :], 1.0, None, ALU.add))
            done(v.reciprocal(cvec[:, 2, :, :], cvec[:, 2, :, :]))
            done(v.tensor_tensor(cvec[:, 0, :, :], cvec[:, 1, :, :], cvec[:, 2, :, :], ALU.mult), v_ready, "silu")

            def modulation(l):
                for n in range(12):
                    dve.wait_ge(*full.at("modT", l, n))
                    bank = bank_of("modT", l, n)[:, 0:8].rearrange("p (c s) -> p c s", c=4)
                    b = cols[:, l, C_BMOD + 4 * n:C_BMOD + 4 * n + 4].unsqueeze(2).to_broadcast([P, 4, 2])
                    done(v.tensor_tensor(modT[:, 4 * n:4 * n + 4, :], bank, b, ALU.add), read_v, "modT", l, n)
                for a, at, g in ((amix, 8, C_GMIX), (affn, 32, C_GFFN)):
                    done(v.tensor_scalar(a[:, :, :], modT[:, at:at + 8, :], 1.0, math.sqrt(D), ALU.add, ALU.mult))
                    done(v.tensor_tensor(a[:, :, :], a[:, :, :], cols[:, l, g:g + 8].unsqueeze(2).to_broadcast([P, 8, 2]), ALU.mult))
                lam0 = 0.8 - 0.6 * math.exp(-0.3 * l)
                done(v.tensor_scalar(gout[:, 0:2], cols[:, l, C_GOUT:C_GOUT + 2], (1.0 - lam0) * math.sqrt(HD), None, ALU.mult))
                done(v.tensor_scalar(gout[:, 2:8], cols[:, l, C_GOUT + 2:C_GOUT + 8], math.sqrt(HD), None, ALU.mult))
                dve.wait_ge(*rows_in.at(l))
                lv = rows[:, R_LAM:R_LAM + 128].rearrange("p (a b d) -> p a b d", a=2, b=2)
                lp = lam[:, 0:64].rearrange("p (a d) -> p a d", a=2)
                done(v.tensor_tensor(lp, lv[:, :, 0, :], lv[:, :, 1, :], ALU.mult))
                done(v.tensor_reduce(lam[:, 64:66], lp, X, ALU.add), v_ready, "lam", l)
                dve.wait_ge(*s_ready.at("lam", l))
                done(v.tensor_tensor(neglam[:, :], lam[:, 67:68], lam[:, 66:67], ALU.subtract))
                done(v.tensor_scalar(neglam[:, :], neglam[:, :], -lam0, None, ALU.add))
                done(v.tensor_scalar(negsink[:, :], rows[:, R_SINK:R_SINK + 4], -1.0, None, ALU.mult))
                for a, b, d in ((0, 512, 32), (512, QK_W, 64)):
                    done(v.tensor_scalar(rows[:, a:b], rows[:, a:b], math.sqrt(d), None, ALU.mult))

            def filters(l):
                dve.wait_ge(*filt_in.at(l))
                done(v.memset(fh[64:65, :], 1.0))
                for n in (1, 2):
                    dve.wait_ge(*full.at(f"fh{n}", l))
                    done(v.tensor_scalar(fr, bank_of(f"fh{n}", l)[0:64, 0:SEQ], fcol[:, l, n - 1:n], fcol[:, l, 2:3],
                                         ALU.add, ALU.mult), read_v, f"fh{n}", l)
                    done(v.tensor_scalar(fn, fr, 1.0 / (2 * math.pi), MAGIC, ALU.mult, ALU.add))
                    done(v.tensor_scalar(fn, fn, MAGIC, None, ALU.subtract))
                    done(v.scalar_tensor_tensor(fr, fn, -6.28125, fr, ALU.mult, ALU.add))
                    done(v.scalar_tensor_tensor(fr, fn, -(2 * math.pi - 6.28125), fr, ALU.mult, ALU.add))
                    done(v.tensor_scalar(fr, fr, 3.1415925, -3.1415925, ALU.min, ALU.max), v_ready, f"fr{n}", l)
                for t in range(TT):
                    for h in range(2):
                        dve.wait_ge(*full.at("filt", l, t, h))
                        done(v.tensor_tensor(filt[:, t, 2 * h:2 * h + 2, :],
                                             bank_of("filt", l, t, h)[:, :].rearrange("p (o n) -> p o n", o=2),
                                             decay[:, t:t + 1, :].to_broadcast([P, 2, SEQ]), ALU.mult),
                             read_v, "filt", l, t, h)
                dve.wait_ge(*full.at("fnorm", l))
                done(v.reciprocal(rnorm[:, :], bank_of("fnorm", l)[:, 0:4]), read_v, "fnorm", l)

            def norm(which, l, s):
                xs = xT[:, :, s * SEQ:(s + 1) * SEQ]
                sqv = sq.rearrange("p (k n) -> p k n", k=KC)
                if which == "mix":
                    dve.wait_ge(*read_s.at("spec", l, NFB - 1))
                    if (l, s) != (0, CTX):
                        pl, ps = passes[passes.index((l, s)) - 1]
                        dve.wait_ge(*(full.at("yT", pl, ps, TT - 1, 1) if is_full(pl, ps) else full.at("qkT", pl, ps, TT - 1, 3)))
                else:
                    dve.wait_ge(*full.at("out", l, s, D // CW - 1))
                done(v.tensor_tensor(sqv, xs, xs, ALU.mult), v_ready, "sq", which, l, s)
                dve.wait_ge(*full.at("norm", which, l, s))
                done(v.tensor_copy(rstd[:, :], bank_of("norm", which, l, s)[:, 0:SEQ]), read_v, "norm", which, l, s)
                root(rstd[:, :], D, sq[:, 0:SEQ], sq[:, SEQ:2 * SEQ])
                done(v.tensor_tensor(hT[:, :, :], xs, rstd[:, :].unsqueeze(1).to_broadcast([P, KC, SEQ]), ALU.mult),
                     v_ready, "xn", which, l, s)

            def groups(l, s):
                return ((0, 512, 32), (512, QK_W, 64)) if is_full(l, s) else ((256, 512, 32), (1024, QK_W, 64))

            def qk(l, s):
                dve.wait_ge(*read_s.at("in", l, s, WGK))
                for r, (a, b, d) in enumerate(groups(l, s)):
                    n = (b - a) // d
                    for t in range(TT):
                        x = ptok[:, t, a:b]
                        x4, q4, r4 = (z.rearrange("p (h d) -> p h d", d=d) for z in (x, qk_a[:, a:b], qk_b[:, a:b]))
                        st = stat[:, 0:n]
                        done(v.tensor_tensor(qk_a[:, a:b], x, x, ALU.mult))
                        done(v.tensor_reduce(st, q4, X, ALU.add))
                        root(st, d, qk_b[:, 0:n], qk_b[:, n:2 * n])
                        done(v.tensor_tensor(x4, x4, st.unsqueeze(2).to_broadcast([P, n, d]), ALU.mult))
                        done(v.tensor_tensor(x, x, rows[:, a:b], ALU.mult))
                        if s == CTX:
                            continue
                        h = d // 2
                        tc, ts = (T_C32, T_S32) if d == 32 else (T_C64, T_S64)
                        cos = tab[:, t, tc:tc + h].unsqueeze(1).to_broadcast([P, n, h])
                        sin = tab[:, t, ts:ts + h].unsqueeze(1).to_broadcast([P, n, h])
                        lo, hi = slice(0, h), slice(h, d)
                        done(v.tensor_tensor(q4[:, :, lo], x4[:, :, lo], cos, ALU.mult))
                        done(v.tensor_tensor(q4[:, :, hi], x4[:, :, hi], cos, ALU.mult))
                        done(v.tensor_tensor(r4[:, :, lo], x4[:, :, hi], sin, ALU.mult))
                        done(v.tensor_tensor(r4[:, :, hi], x4[:, :, lo], sin, ALU.mult))
                        done(v.tensor_tensor(x4[:, :, lo], q4[:, :, lo], r4[:, :, lo], ALU.subtract))
                        done(v.tensor_tensor(x4[:, :, hi], q4[:, :, hi], r4[:, :, hi], ALU.add))
                v_step.also("qk", l, s)

            def attention(l, s):
                units = [(t, h) for t in range(TT) for h in range(12)]
                nk = SEQ if s == CTX else 2 * SEQ

                def probs(t, h):
                    return s_ready.at("sinke", l, s, t, h) if 4 <= h < 8 else read_s.at("s", l, s, t, h, int(h < 4))

                def maxima(t, h):
                    i = (t * 12 + h) % 2
                    scale = (32 if h < 4 else 64) ** -0.5
                    for c in range(2 if h < 4 else 1):
                        dve.wait_ge(*full.at("s", l, s, t, h, c))
                        bank = bank_of("s", l, s, t, h, c)
                        if 4 <= h < 8 and s == LAT:
                            far = bank[:, SEQ + (1 - t) * P:SEQ + (2 - t) * P]
                            m = tab[:, t, T_MASK:T_MASK + P]
                            done(v.tensor_tensor(far, far, m, ALU.add))
                        done(v.tensor_reduce(mx[:, i, c:c + 1], bank[:, 0:nk], X, ALU.max))
                        if 4 <= h < 8:
                            done(v.tensor_scalar(negm[:, i, c:c + 1], mx[:, i, c:c + 1], -scale, negsink[:, h - 4:h - 3],
                                                 ALU.mult, ALU.min), v_ready, "negm", l, s, t, h, c)
                        else:
                            done(v.tensor_scalar(negm[:, i, c:c + 1], mx[:, i, c:c + 1], -scale, None,
                                                 ALU.mult), v_ready, "negm", l, s, t, h, c)

                def sums(t, h):
                    i, z = (t * 12 + h) % 2, (t * 12 + h) % 8
                    dve.wait_ge(*probs(t, h))
                    if 4 <= h < 8:
                        done(v.tensor_tensor(zsum[:, z, 0:1], zsum[:, z, 0:1], sinke[:, i:i + 1], ALU.add))
                    n = 2 if h < 4 else 1
                    done(v.reciprocal(rz[:, z, 0:n], zsum[:, z, 0:n]))
                    if h < 4:
                        done(v.tensor_tensor(rz[:, z, 1:2], rz[:, z, 1:2], neglam[:, :], ALU.mult))
                        done(v.tensor_scalar(prob[:, i, 0, 0:nk], prob[:, i, 0, 0:nk], rz[:, z, 0:1], None, ALU.mult))
                        done(v.scalar_tensor_tensor(prob[:, i, 0, 0:nk], prob[:, i, 1, 0:nk], rz[:, z, 1:2],
                                                    prob[:, i, 0, 0:nk], ALU.mult, ALU.add), v_ready, "prob", l, s, t, h)

                def outputs(t, h):
                    if h % 4 < 3:
                        return
                    z = (t * 12 + h - 3) % 8
                    dve.wait_ge(*full.at("o", l, s, t, h))
                    src = obank[:, 0:4 * HD].rearrange("p (h d) -> p h d", d=HD)
                    dst = otok[:, t, HD * (h - 3):HD * (h + 1)].rearrange("p (h d) -> p h d", d=HD)
                    if h < 4:
                        done(v.tensor_copy(dst, src), read_v, "o", l, s, t, h)
                    else:
                        done(v.tensor_tensor(dst, src, rz[:, z:z + 4, 0:1].to_broadcast([P, 4, HD]), ALU.mult),
                             read_v, "o", l, s, t, h)

                n = len(units)
                for i in range(n + 2):
                    if i < n:
                        if i >= 2:
                            dve.wait_ge(*probs(*units[i - 2]))
                        maxima(*units[i])
                    if 1 <= i <= n:
                        sums(*units[i - 1])
                    if i >= 2:
                        outputs(*units[i - 2])
                o4 = otok[:, :, :].rearrange("p t (h d) -> p t h d", d=HD)
                st = stat[:, 0:24].rearrange("p (t n) -> p t n", t=TT)
                done(v.tensor_tensor(osq, o4, o4, ALU.mult))
                done(v.tensor_reduce(st, osq, X, ALU.add))
                root(stat[:, 0:24], HD, qk_a[:, 0:24], qk_a[:, 24:48])
                done(v.tensor_tensor(o4, o4, st.unsqueeze(3).to_broadcast([P, TT, 12, HD]), ALU.mult), v_ready, "onorm", l, s)

            def hyena(l, s):
                dve.wait_ge(*read_s.at("in", l, s, N_IN - 1))
                for c in range(6):
                    w = [cols[:, l, C_CONVW + 6 * i + c:C_CONVW + 6 * i + c + 1] for i in range(3)]
                    b = cols[:, l, C_CONVB + c:C_CONVB + c + 1]
                    done(v.tensor_scalar(uc[:, c, :], upad[:, c, 1:SEQ + 1], w[1], b, ALU.mult, ALU.add))
                    done(v.scalar_tensor_tensor(uc[:, c, :], upad[:, c, 0:SEQ], w[0], uc[:, c, :], ALU.mult, ALU.add))
                    done(v.scalar_tensor_tensor(uc[:, c, :], upad[:, c, 2:SEQ + 2], w[2], uc[:, c, :], ALU.mult, ALU.add),
                         *((v_ready, "z", l, s, 0) if c == 5 else (v_step,)))
                for o in range(2):
                    dve.wait_ge(*full.at("zf", l, s, o, 0))
                    dve.wait_ge(*full.at("zf", l, s, o, 1))
                    re, im = (bank_of("zf", l, s, o, r)[:, :].rearrange("p (b n) -> p b n", b=2) for r in range(2))
                    t1, t2 = hy[:, 4:6, :], hy[:, 6:8, :]
                    done(v.tensor_tensor(t1, re, spec[:, 0:2, o, :], ALU.mult))
                    done(v.tensor_tensor(t2, im, spec[:, 2:4, o, :], ALU.mult))
                    done(v.tensor_tensor(yspec[:, 0:2, :], t1, t2, ALU.subtract))
                    done(v.tensor_tensor(t1, re, spec[:, 2:4, o, :], ALU.mult), read_v, "zf", l, s, o, 0)
                    done(v.tensor_tensor(t2[:, 0:1, :], im[:, 0:1, :], spec[:, 4:5, o, :], ALU.mult))
                    done(v.tensor_tensor(t2[:, 1:2, :], im[:, 1:2, :], spec[:, 1:2, o, :], ALU.mult), read_v, "zf", l, s, o, 1)
                    done(v.tensor_tensor(yspec[:, 2:4, :], t1, t2, ALU.add), v_ready, "yspec", l, s, o)
                    dve.wait_ge(*full.at("y", l, s, o))
                    y = bank_of("y", l, s, o)[:, :].rearrange("p (c n) -> p c n", c=2)
                    for c in range(2):
                        z = uc[:, c, :] if o == 0 else hy[:, c, :]
                        hb = cols[:, l, C_HYB + 2 * o + c:C_HYB + 2 * o + c + 1]
                        done(v.tensor_scalar(z, z, hb, None, ALU.mult))
                        done(v.scalar_tensor_tensor(z, y[:, c, :], rnorm[:, 2 * o + c:2 * o + c + 1], z, ALU.mult, ALU.add),
                             *((read_v, "y", l, s, o) if c == 1 else (v_step,)))
                        done(v.tensor_tensor(hy[:, c, :], z, uc[:, 2 + 2 * o + c, :], ALU.mult),
                             *((v_ready, "z", l, s, 1) if c == 1 and o == 0 else (v_step,)))
                done(v.tensor_tensor(hy[:, 2:4, :], hy[:, 0:2, :], hy[:, 0:2, :], ALU.mult), v_ready, "hysq", l, s)
                dve.wait_ge(*full.at("hynorm", l, s))
                bank = bank_of("hynorm", l, s)[:, :].rearrange("p (c n) -> p c n", c=2)
                done(v.tensor_copy(hy[:, 4:6, :], bank), read_v, "hynorm", l, s)
                root(hy[:, 4:6, :], HD, hy[:, 6:8, :], hy[:, 2:4, :])
                for c in range(2):
                    done(v.scalar_tensor_tensor(mixT[:, 6 + c, :], hy[:, c, :], gout[:, 6 + c:7 + c], hy[:, 4 + c, :],
                                                ALU.mult, ALU.mult),
                         *((v_ready, "mixT", l, s) if c else (v_step,)))

            def out_proj(l, s):
                for j in range(D // CW):
                    dve.wait_ge(*full.at("out", l, s, j))
                    for i in range(2):
                        c = 2 * j + i
                        xs = xT[:, c, s * SEQ:(s + 1) * SEQ]
                        done(v.scalar_tensor_tensor(xs, bank_of("out", l, s, j)[:, i * SEQ:(i + 1) * SEQ],
                                                    modT[:, 16 + c, s:s + 1], xs, ALU.mult, ALU.add),
                             *((read_v, "out", l, s, j) if i else (v_step,)))

            def top16(src, tmp, vals, ids):
                done(v.max(vals[:, 0:8], src))
                done(v.max_index(ids[:, 0:8], vals[:, 0:8], src))
                done(v.match_replace(tmp, vals[:, 0:8], src, -3.0e38))
                done(v.max(vals[:, 8:16], tmp))

            def candidates(l, s, h):
                dve.wait_ge(*full.at("ks", l, s, h))
                bank = bank_of("ks", l, s, h)
                for t in range(TT):
                    for half in range(2):
                        i = 2 * t + half
                        ids = idx_a[:, t, half, h, :]
                        top16(bank[:, i * P:(i + 1) * P], work, top8[:, i, :], ids)
                        done(v.max_index(ids[:, 8:16], top8[:, i, 8:16], work),
                             *((read_v, "ks", l, s, h) if i == 3 else (v_step,)))
                    c3 = cand.rearrange("p (a b) -> p a b", a=TOPK)
                    done(v.tensor_tensor(c3, top8[:, 2 * t, :].unsqueeze(2).to_broadcast([P, TOPK, TOPK]),
                                         top8[:, 2 * t + 1, :].unsqueeze(1).to_broadcast([P, TOPK, TOPK]), ALU.add))
                    top16(cand, cand2, best[:, t, h, :], pos[:, t, h, :])
                    done(v.max_index(pos[:, t, h, 8:16], best[:, t, h, 8:16], cand2))

            def route(l, s, t):
                g3 = gate[:, t, :].rearrange("p (h k) -> p h k", h=HEADS)
                bt = best[:, t, :, :]
                done(v.tensor_tensor(g3, bt, bt[:, :, 0:1].to_broadcast([P, HEADS, TOPK]), ALU.subtract),
                     v_ready, "best", l, s, t)
                pv = pos[:, t, :, :].rearrange("p h k -> p (h k)")
                done(v.tensor_scalar(pij[:, 0, :], pv, 4, None, ALU.logical_shift_right))
                done(v.tensor_scalar(pij[:, 1, :], pv, 15, None, ALU.bitwise_and))
                done(v.tensor_copy(pijf[:, :, :], pij[:, :, :]))
                done(v.tensor_copy(idx_f[:, :, :, :], idx_a[:, t, :, :, :]))
                hot3 = hot.rearrange("p (e i) -> p e i", i=TOPK)
                hot4 = hot.rearrange("p (h k i) -> p h k i", h=HEADS, i=TOPK)
                for a in range(2):
                    done(v.tensor_tensor(hot3, pijf[:, a, :].unsqueeze(2).to_broadcast([P, NE, TOPK]),
                                         iota16[:, :].unsqueeze(1).to_broadcast([P, NE, TOPK]), ALU.is_equal))
                    done(v.tensor_tensor(hot4, hot4, idx_f[:, a, :, :].unsqueeze(2).to_broadcast([P, HEADS, TOPK, TOPK]), ALU.mult))
                    done(v.tensor_reduce(eij[:, a, :], hot3, X, ALU.add))
                done(v.scalar_tensor_tensor(eij[:, 0, :], eij[:, 0, :], float(N_KEYS), eij[:, 1, :], ALU.mult, ALU.add))
                if l:
                    done(v.tensor_scalar(eij[:, 0, :], eij[:, 0, :], float(l * N_EXPERTS), None, ALU.add))
                done(v.tensor_copy(expert[:, t, :], eij[:, 0, :]), v_ready, "expert", l, s, t)
                dve.wait_ge(*s_ready.at("gate", l, s, t))
                done(v.tensor_reduce(gz[:, 0, :], g3, X, ALU.add))
                done(v.reciprocal(gz[:, 1, :], gz[:, 0, :]))
                done(v.tensor_scalar(gz[:, 1, :], gz[:, 1, :], 0.5, None, ALU.mult))
                done(v.tensor_tensor(g3, g3, gz[:, 1, :].unsqueeze(2).to_broadcast([P, HEADS, TOPK]), ALU.mult))

            def experts(l, s, t):
                q = peer_tiles.index((l, s, t))
                if t == 0:
                    dve.wait_ge(*read_s.at("h2", l, s, TT - 1, 1))
                with dve.Fori(q * STEPS // 2, (q + 1) * STEPS // 2) as i:
                    for g in range(2):
                        x, pol, w = dots[:, g, :], poly[:, g, :], wexp[:, g, :]
                        for j in range(STEP):
                            dve.wait_ge(u_in[j].sem, i * 32 + (16 * g + 16))
                            v.tensor_tensor_reduce(urow[:, j, :], urow[:, j, :], h2tok[:, t, :], 1.0, 0.0,
                                                   ALU.mult, ALU.add, x[:, j:j + 1]).then_inc(u_used.sem, 1)
                        dve.wait_ge(u_used.sem, i * 2 * STEP + (STEP * (g + 1) + U_0))
                        v.tensor_tensor(pol, x, x, ALU.mult).then_inc(gelu_step.sem, 1)
                        dve.wait_ge(gelu_step.sem, i * 6 + (3 * g + 1))
                        v.tensor_scalar(pol, pol, GELU_C, 1.0, ALU.mult, ALU.add).then_inc(gelu_step.sem, 1)
                        dve.wait_ge(gelu_step.sem, i * 6 + (3 * g + 2))
                        v.tensor_tensor(pol, pol, x, ALU.mult).then_inc(poly_ready.sem, 1)
                        dve.wait_ge(th_ready.sem, i * 2 + (g + 1))
                        v.scalar_tensor_tensor(th[:, g, :], th[:, g, :], 1.0, x, ALU.add, ALU.mult).then_inc(gelu_step.sem, 1)
                        dve.wait_ge(gelu_step.sem, i * 6 + (3 * g + 3))
                        dve.wait_ge(diag_ready.sem, i * 2 * STEP + (STEP * (g - 1) + DIAG_0))
                        v.tensor_tensor(w, th[:, g, :], gate[:, t, bass.ds(i * 2 * STEP + (STEP * g - q * NE), STEP)],
                                        ALU.mult).then_inc(w_ready.sem, 1)
                        dve.wait_ge(w_ready.sem, i * 2 + (g + 1))

            def add_experts(l, s, t):
                for g in range(2):
                    dve.wait_ge(*full.at("yT", l, s, t, g))
                    for i in range(4):
                        c = 4 * g + i
                        xs = xT[:, c, s * SEQ + t * P:s * SEQ + (t + 1) * P]
                        done(v.scalar_tensor_tensor(xs, bank_of("yT", l, s, t, g)[:, i * P:(i + 1) * P],
                                                    modT[:, 40 + c, s:s + 1], xs, ALU.mult, ALU.add),
                             v_ready, "x_ffn", l, s, t, c)
                    v_ready.also("yT", l, s, t, g)

            for l in range(DEPTH):
                modulation(l)
                filters(l)
                for s in (CTX, LAT):
                    norm("mix", l, s)
                    qk(l, s)
                    if is_full(l, s):
                        attention(l, s)
                        hyena(l, s)
                        out_proj(l, s)
                        norm("ffn", l, s)
                        for h in range(HEADS):
                            candidates(l, s, h)
                        for t in range(TT):
                            route(l, s, t)
                        for t in range(TT):
                            experts(l, s, t)
                            add_experts(l, s, t)

        @block.gpsimd
        def _(pool):
            for q, (l, s, t) in enumerate(peer_tiles):
                ready = v_ready.at("expert", l, s, t)

                def u_step(i, b):
                    pool.wait_ge(v_used.sem, i * STEP + (V_0 - IXB * STEP + STEP))
                    pool.wait_ge(*ready)
                    nc.gpsimd.tensor_copy(ix[:, b, :], expert[:, t, bass.ds(i * STEP + (-q * NE), STEP)]).then_inc(ix_ready.sem, 1)
                    pool.wait_ge(ix_ready.sem, i + 1)
                    pool.sem_inc(row_free.sem, 1)
                    for j in range(STEP):
                        pool.wait_ge(u_used.sem, i * STEP + (j + 1 - STEP + U_0))
                        pool.sem_inc(row_free.sem, 1)
                        pool.indirect_dma_start(urow[:, j, :], None, dram["u"],
                                                bass.IndirectOffsetOnAxis(ap=ix[:, b, j:j + 1], axis=0)).then_inc(u_in[j].sem, 16)

                def v_step_(i, b):
                    for j in range(STEP):
                        pool.wait_ge(v_used.sem, i * STEP + (j + 1 - STEP + V_0))
                        pool.sem_inc(row_free.sem, 1)
                        pool.indirect_dma_start(vrow[:, j, :], None, dram["v"],
                                                bass.IndirectOffsetOnAxis(ap=ix[:, b, j:j + 1], axis=0)).then_inc(v_in[j].sem, 16)

                at = q * STEPS
                u_step(at, 0)
                with pool.Fori(at, at + STEPS - IXB, IXB) as i:
                    for b in range(IXB):
                        u_step(i + (b + 1), (b + 1) % IXB)
                        v_step_(i + b, b)
                for b in range(IXB):
                    if b < IXB - 1:
                        u_step(at + STEPS - IXB + b + 1, b + 1)
                    v_step_(at + STEPS - IXB + b, b)

        ledger["bank_order"] = list(taken)


def constants():
    n = np.arange(SEQ, dtype=np.float64)
    f = np.arange(SEQ, dtype=np.float64)
    w = 2 * np.pi / 512
    re = np.cos(w * np.outer(n, f))
    im = -np.sin(w * np.outer(n, f))
    nyq = np.cos(np.pi * n)
    im_packed = im.copy()
    im_packed[:, 0] = nyq
    dft = np.concatenate([re, im_packed], 1)
    ire = np.cos(w * np.outer(f, n)) * 2 / 512
    ire[0] /= 2
    iim = -np.sin(w * np.outer(f, n)) * 2 / 512
    iim[0] = nyq / 512
    idft = np.concatenate([ire, iim], 0)
    def fil(sign):
        r, i = re.copy(), sign * im
        last = r[:, 0:P].copy()
        last[:, 0] = nyq
        m = np.concatenate([r, i, last], 1)
        if sign < 0:
            m[0] = 0
        return m
    fdft = np.concatenate([fil(1.0), fil(-1.0)], 0)
    t = np.linspace(0.0, 1.0, SEQ, dtype=np.float32)[:, None]
    wn = (np.float32(2.0 * math.pi / SEQ) * np.arange(SEQ, dtype=np.float32))[:, None]
    fb = np.linspace(1e-4, BANDS - 1, BANDS, dtype=np.float32)[None, :]
    ang = (fb * wn).astype(np.float64)
    feat = np.concatenate([t, np.cos(ang), -np.sin(ang)], -1)
    deltas = np.abs(np.linspace(math.log(1e-2) / 1.5, math.log(1e-2) / 0.3, SEQ))
    decay = np.exp(-t.astype(np.float64) * deltas)

    def rope(dim):
        pos = np.arange(SEQ)
        axis = dim // 2
        inv = 10000.0 ** (-np.arange(0, axis, 2) / axis)
        a = np.concatenate([(pos // GRID_W)[:, None] * inv, (pos % GRID_W)[:, None] * inv], -1)
        return np.cos(a), np.sin(a)

    (c32, s32), (c64, s64) = rope(32), rope(64)
    q, k = np.arange(P)[:, None], np.arange(P)[None, :]
    mask = np.concatenate([np.where(k <= q, 0.0, -1e30), np.where(k >= q, 0.0, -1e30)], 0)
    tab = np.concatenate([c32, s32, c64, s64, mask], 1)

    def tiles(a):
        return np.ascontiguousarray(a.reshape(-1, P, a.shape[-1]).transpose(1, 0, 2), np.float32)

    half = np.kron(np.eye(2), np.ones((HD, HD)))
    nc_ = np.ones((P, 2))
    nc_[0, 1] = 0
    return {
        "ident": np.eye(P, dtype=np.float32), "half_ones": half.astype(np.float32), "norm_cols": nc_.astype(np.float32),
        "dft": tiles(dft), "idft": tiles(idft), "fdft": tiles(fdft), "decay": tiles(decay),
        "feat": np.ascontiguousarray(feat.T, np.float32), "tab": tiles(tab),
        "iota16": np.ascontiguousarray(np.broadcast_to(np.arange(TOPK, dtype=np.float32), (P, TOPK))),
    }


def layouts(a):
    def chunks(w):
        L, _, n = w.shape
        return np.ascontiguousarray(w.reshape(L, KC, P, n // CW, CW).transpose(0, 3, 2, 1, 4))

    def col(v, n):
        return np.asarray(v).reshape(DEPTH, n, P).transpose(0, 2, 1)

    w = np.asarray(a["w_in"])
    pair = [0, 2, 1, 3]

    def heads(at):
        return [w[:, :, at + h * HD:at + (h + 1) * HD] for h in pair]

    w_in = np.concatenate([w[:, :, 0:256], *heads(768), *heads(1280), w[:, :, 256:512], w[:, :, 1024:1152],
                           w[:, :, 1536:1664], w[:, :, 512:768], w[:, :, 1152:1280], w[:, :, 1664:1792],
                           w[:, :, 1792:2560]], 2)
    cols = np.concatenate([
        col(a["b_mod"], 48), col(a["g_norm_mix"], 8), col(a["g_norm_ffn"], 8), col(a["g_mix_out"], 8),
        col(a["hy_conv_w"], 18), col(a["hy_conv_b"], 6), col(a["hy_bias"], 4)], 2)
    gd, gw, gg = (np.asarray(a[k]) for k in ("g_qk_diff", "g_qk_win", "g_qk_glob"))
    row = np.concatenate([
        np.tile(gd[:, 0], (1, 8)), np.tile(gd[:, 1], (1, 8)), np.tile(gw[:, 0], (1, 4)), np.tile(gg[:, 0], (1, 4)),
        np.tile(gw[:, 1], (1, 2)), np.tile(gg[:, 1], (1, 2)), a["sink_win"], np.asarray(a["lambda_diff"]).reshape(DEPTH, 128)], 1)
    rows = np.ascontiguousarray(np.broadcast_to(row[:, None, :], (DEPTH, P, N_ROWS)))
    cv = np.stack([a["c_ctx"], a["c"][0]], 1).reshape(KC, P, 2).transpose(1, 0, 2)
    keys = np.asarray(a["peer_keys"]).transpose(0, 4, 1, 2, 3).reshape(DEPTH, P, 16, P)
    return {
        "x": a["x"][0].T.reshape(KC, P, SEQ).transpose(1, 0, 2),
        "ctx": a["ctx"][0].T.reshape(KC, P, SEQ).transpose(1, 0, 2),
        "cvec": cv, "cols": cols.transpose(1, 0, 2), "rows": rows,
        "mod": chunks(np.asarray(a["w_mod"])), "in": chunks(w_in), "out": chunks(np.asarray(a["w_out"])),
        "wq": chunks(np.asarray(a["peer_wq"])), "keys": keys,
        "fw1": np.asarray(a["hy_w1"]).transpose(1, 0, 2), "fw2": np.asarray(a["hy_w2"]).transpose(1, 0, 2),
        "fw3": np.concatenate([a["hy_w3"], np.asarray(a["hy_b3"])[:, None, :]], 1),
        "fcol": np.stack([a["hy_b1"], a["hy_b2"], a["hy_freq"]], 2).transpose(1, 0, 2),
        "u": np.asarray(a["peer_u"]).reshape(DEPTH * N_EXPERTS, D), "v": np.asarray(a["peer_v"]).reshape(DEPTH * N_EXPERTS, D),
    }


def kernel(**inputs):
    import concourse.bacc as bacc
    from concourse.bass_utils import run_bass_kernel_spmd

    arrays = {n: np.asarray(v) for n, v in inputs.items()}
    arrays = {n: np.ascontiguousarray(v) for n, v in {**constants(), **layouts(arrays)}.items()}
    ledger = {}
    for _ in range(2):
        nc = bacc.Bacc("TRN2", target_bir_lowering=False, num_devices=1)
        dram = {n: nc.dram_tensor(f"in_{n}_dram", v.shape, F32, kind="ExternalInput").ap() for n, v in arrays.items()}
        dram["y"] = nc.dram_tensor("out_0_dram", (D, SEQ), F32, kind="ExternalOutput").ap()
        build(nc, dram, ledger)
    r = run_bass_kernel_spmd(nc, [{f"in_{n}_dram": v for n, v in arrays.items()}], core_ids=[0])
    return np.ascontiguousarray(r.results[0]["out_0_dram"].T)[None]
```

```python
import math
from contextlib import ExitStack

import concourse.bass as bass
import numpy as np
from concourse import mybir

F32 = mybir.dt.float32
U32 = mybir.dt.uint32
I32 = mybir.dt.int32
ALU = mybir.AluOpType
ACT = mybir.ActivationFunctionType
X = mybir.AxisListType.X

P = 128
D = 1024
KC = D // P
DEPTH = 2
SEQ = 256
TT = SEQ // P
HD = 64
EPS = 1e-6
CW = 256
N_MOD = 6
GRID_W = 64
BANDS = 16
CTX, LAT = 0, 1

DQ, WQ, GQ, DK, WGK, DV, WGV, HY0 = range(8)
N_IN = 10
QK_AT = {DQ: 0, DK: 256, WQ: 512, GQ: 768, WGK: 1024}
QK_W = 1280

HEADS = 8
N_KEYS = 128
N_EXPERTS = N_KEYS * N_KEYS
TOPK = 16
NE = HEADS * TOPK
STEP = 4
STEPS = NE // STEP
UR = VR = STEP
IXB = 4

C_BMOD, C_GMIX, C_GFFN, C_GOUT, C_CONVW, C_CONVB, C_HYB, N_COLS = 0, 48, 56, 64, 72, 90, 96, 100
R_GQK, R_SINK, R_LAM, N_ROWS = 0, QK_W, QK_W + 4, QK_W + 4 + 128
T_C32, T_S32, T_C64, T_S64, T_MASK, N_TAB = 0, 16, 32, 64, 96, 224
NFB = 5
SCR = 5120
BANKS = 5
MAGIC = 1.5 * 2.0 ** 23
GELU_C = 0.044715
GELU_S = math.sqrt(2.0 / math.pi)


class Signal:

    def __init__(self, sem, name, ledger, step=1):
        self.sem, self.step, self.n = sem, step, 0
        self.counts = ledger.setdefault(name, {})

    def mark(self, *event):
        self.n += self.step
        self.counts[event or (self.n,)] = self.n
        return self.sem, self.step

    def also(self, *event):
        self.counts[event] = self.n

    def at(self, *event):
        return self.sem, self.counts.get(event, 1)

    def knows(self, *event):
        return event in self.counts


def weight_order():
    order = []
    for l in range(DEPTH):
        order += [("mod", l, j) for j in range(N_MOD * D // CW)]
        for s in (CTX, LAT):
            full = s == LAT or l < DEPTH - 1
            order += [("in", l, j, s) for j in (range(N_IN) if full else (DK, WGK, DV, WGV))]
            if full:
                order += [("out", l, j, s) for j in range(D // CW)]
                order += [("wq", l, j, s) for j in range(HEADS)]
    return order


WS = 3


def product_of(kind, l, j, s=None):
    if kind == "mod":
        return ("mod", l, j // 2) if j % 2 else ("modhalf", l, j // 2)
    return {"in": "in", "out": "out", "wq": "pq"}[kind], l, s, j


def build(nc, dram, ledger):
    ctx = ExitStack()
    with ctx:
        def sb(name, shape, dt=F32):
            return ctx.enter_context(nc.sbuf_tensor(name, shape, dt))

        def signal(name, step=1):
            return Signal(ctx.enter_context(nc.semaphore(name)), name, ledger, step)

        xT = sb("xT", [P, KC, 2 * SEQ])
        hT = sb("hT", [P, KC, SEQ])
        ident = sb("ident", [P, P])
        ones = sb("ones", [P, P])
        zeros = sb("zeros", [P, P])
        half_ones = sb("half_ones", [P, P])
        norm_cols = sb("norm_cols", [P, 2])
        dft = sb("dft", [P, TT, 512])
        idft = sb("idft", [P, 4, SEQ])
        tab = sb("tab", [P, TT, N_TAB])
        cols = sb("cols", [P, DEPTH, N_COLS])
        rows = sb("rows", [P, N_ROWS])
        w_sb = sb("w_sb", [P, WS, KC, CW])
        cvec = sb("cvec", [P, 3, KC, 2])
        modT = sb("modT", [P, DEPTH, 48, 2])
        amix = sb("amix", [P, DEPTH, KC, 2])
        affn = sb("affn", [P, DEPTH, KC, 2])
        gout = sb("gout", [P, KC])
        lam = sb("lam", [P, 64 + 8])
        neglam = sb("neglam", [P, 1])
        negsink = sb("negsink", [P, 4])
        rstd = sb("rstd", [P, SEQ])
        spec = sb("spec", [P, NFB, 2, SEQ])
        rnorm = sb("rnorm", [P, 4])
        fw1 = sb("fw1", [2 * BANDS + 1, DEPTH, 64])
        fw2 = sb("fw2", [64, DEPTH, 64])
        fcol = sb("fcol", [64, DEPTH, 3])
        scratch = sb("scratch", [P, SCR])
        qT = sb("qT", [P, 6, SEQ])
        kT = sb("kT", [P, 4, 2 * SEQ])
        vtok = sb("vtok", [P, 2 * TT, 512])
        stat = sb("stat", [P, 56 + 24])
        prob = sb("prob", [P, 2, 2, 2 * SEQ])
        probT = sb("probT", [P, 2, 4, P])
        mx = sb("mx", [P, 2, 2])
        negm = sb("negm", [P, 2, 2])
        zsum = sb("zsum", [P, 8, 2])
        sinke = sb("sinke", [P, 2])
        rz = sb("rz", [P, 8, 2])
        mixT = sb("mixT", [P, KC, SEQ])
        upad = sb("upad", [P, 6, SEQ + 2])
        zy = sb("zy", [P, 1536])
        otok = zy[:, :].rearrange("p (t n) -> p t n", t=TT)
        zt = zy[:, 0:512].rearrange("p (t n) -> p t n", t=TT)
        yspec = zy[:, 512:1536].rearrange("p (t n) -> p t n", t=4)
        h2tok = sb("h2tok", [P, TT, D])
        top8 = sb("top8", [P, 4, TOPK])
        idx_a = sb("idx_a", [P, TT, 2, HEADS, TOPK], U32)
        best = sb("best", [P, TT, HEADS, TOPK])
        pos = sb("pos", [P, TT, HEADS, TOPK], U32)
        gz = sb("gz", [P, 2, HEADS])
        gate = sb("gate", [P, 2, TT, NE])
        expert = sb("expert", [P, 2, TT, NE], U32)
        ix = sb("ix", [P, IXB, STEP], U32)
        urow = sb("urow", [P, UR, D])
        vrow = sb("vrow", [P, VR, D])
        dots = sb("dots", [P, 2, STEP])
        poly = sb("poly", [P, 2, STEP])
        th = sb("th", [P, 2, STEP])
        wexp = sb("wexp", [P, 2, STEP])
        diag = sb("diag", [P, VR, P])
        iota16 = sb("iota16", [P, TOPK])

        ptok = scratch[:, 0:2 * QK_W].rearrange("p (t n) -> p t n", t=TT)
        qk_a = scratch[:, 2 * QK_W:3 * QK_W]
        qk_b = scratch[:, 3 * QK_W:4 * QK_W]
        osq = scratch[:, 2 * QK_W:2 * QK_W + TT * 768].rearrange("p (t h d) -> p t h d", t=TT, d=HD)
        uc = scratch[:, 0:1536].rearrange("p (c n) -> p c n", c=6)
        hy = scratch[:, 1536:1536 + 2048].rearrange("p (c n) -> p c n", c=8)
        sq = scratch[:, 2560:2560 + 2048]
        fdft = scratch[:, 0:4 * NFB * P].rearrange("p (k n) -> p k n", k=4)
        filt = mixT[:, :, :].rearrange("p k n -> p (k n)").rearrange("p (t o n) -> p t o n", t=TT, o=4)
        afilt = vtok[:, :, :].rearrange("p k n -> p (k n)").rearrange("p (t o n) -> p t o n", t=TT, o=4)
        decay = scratch[:, 2560:2560 + 512].rearrange("p (t n) -> p t n", t=TT)
        feat = scratch[0:2 * BANDS + 1, 3072:3072 + SEQ]
        fh = scratch[0:65, 3328:3328 + SEQ]
        fn = scratch[0:64, 3584:3584 + SEQ]
        fr = scratch[0:64, 3840:3840 + SEQ]
        fw3 = zy[0:65, 0:1024]
        modrow = scratch[0:2, 4096:5120].rearrange("p (b n) -> p b n", b=2)
        hot = scratch[:, 0:2048]
        cand = scratch[:, 2048:2304]
        cand2 = scratch[:, 2304:2560]
        work = scratch[:, 4608:4608 + P]
        pq = scratch[:, 2560:3584].rearrange("p (a b n) -> p a b n", a=2, b=2)
        pij = scratch[:, 3584:3840].rearrange("p (a n) -> p a n", a=2).bitcast(U32)
        pijf = scratch[:, 3840:4096].rearrange("p (a n) -> p a n", a=2)
        idx_f = scratch[:, 4096:4352].rearrange("p (a h k) -> p a h k", a=2, h=HEADS)
        eij = scratch[:, 4352:4608].rearrange("p (a n) -> p a n", a=2)
        keys = mixT[:, :, :].rearrange("p k n -> p (k n)").rearrange("p (c n) -> p c n", c=16)

        banks = [ctx.enter_context(nc.psum_tensor(f"bank{i}", [P, 512], F32)) for i in range(BANKS)]
        obank = ctx.enter_context(nc.psum_tensor("obank", [P, 512], F32))
        acc = [ctx.enter_context(nc.psum_tensor(f"acc{i}", [P, 512], F32)) for i in range(2)]

        consts_in = signal("consts_in", 16)
        rows_in = signal("rows_in", 16)
        filt_in = signal("filt_in", 16)
        keys_in = signal("keys_in", 16)
        weights_in = [signal(f"weights_in{i}", 16) for i in range(WS)]
        full = signal("full")
        read_v = signal("read_v")
        read_s = signal("read_s")
        v_step = signal("v_step")
        s_step = signal("s_step")
        v_ready = signal("v_ready")
        s_ready = signal("s_ready")
        p_ready = signal("p_ready")
        u_in = [signal(f"u_in{i}", 16) for i in range(UR)]
        v_in = [signal(f"v_in{i}", 16) for i in range(VR)]
        ix_ready = signal("ix_ready")
        u_used = signal("u_used")
        row_free = signal("row_free")
        poly_ready = signal("poly_ready")
        th_ready = signal("th_ready")
        w_ready = signal("w_ready")
        diag_ready = signal("diag_ready")
        v_used = signal("v_used")
        out_done = signal("out_done", 16)
        gelu_step = signal("gelu_step")

        bank_order = ledger.setdefault("bank_order", [])
        taken = []

        index_of = {k: i for i, k in enumerate(bank_order)}

        def bank_of(*key):
            return banks[index_of.get(key, 0) % BANKS]

        def emptied(key):
            return next((x.at(*key) for x in (read_v, v_ready, read_s) if x.knows(*key)), read_s.at(*key))

        passes = [(l, s) for l in range(DEPTH) for s in (CTX, LAT)]

        def is_full(l, s):
            return s == LAT or l < DEPTH - 1

        peer_tiles = [(l, s, t) for l, s in passes if is_full(l, s) for t in range(TT)]
        U_0, DIAG_0, V_0 = STEP, 2 * STEP, IXB * STEP

        labels = {}

        def run(engine, work):
            for label in work:
                labels.setdefault(engine, []).append(label)

        def experts(engine, eng, l, s, work, f):
            alive = True
            lag = int(engine == "PE")
            for t in range(TT):
                f["expert_start"](l, s, t)
                at = peer_tiles.index((l, s, t)) * STEPS
                n = 0
                while alive and n < STEPS:
                    if n >= lag:
                        f["expert_steps"](l, s, t, at + n - lag, 1)
                    n += 1
                    label = next(work, None)
                    labels.setdefault(engine, []).append(label)
                    alive = label is not None
                if n and lag:
                    f["expert_steps"](l, s, t, at + n - lag, 1)
                if n % 2:
                    f["expert_steps"](l, s, t, at + n, 1)
                    n += 1
                if n < STEPS:
                    with eng.Fori((at + n) // 2, (at + STEPS) // 2) as i:
                        f["expert_steps"](l, s, t, i, 2)
                f["expert_end"](l, s, t)
            run(engine, work)

        def wait_qk():
            for r in range(2):
                for t in range(TT):
                    yield "qk", r, t

        def layer_start(l, f):
            yield from f["modulation"](l)
            yield from f["filters"](l)

        def mixing(l, s, f):
            yield from f["mix_norm"](l, s)
            yield from f["in_proj"](l, s)
            if "qk" in f:
                yield from f["qk"](l, s)
            yield from f["turn_qk"](l, s)
            if is_full(l, s):
                for stage in ("attention", "turn_o", "hyena", "out_proj", "ffn_norm", "peer_queries"):
                    if stage in f:
                        yield from f[stage](l, s)

        def during_latent(l, f):
            if l + 1 < DEPTH:
                yield from layer_start(l + 1, f)
                yield from mixing(l + 1, CTX, f)

        def whole(engine, eng, f):
            run(engine, layer_start(0, f))
            run(engine, mixing(0, CTX, f))
            for l in range(DEPTH):
                if is_full(l, CTX):
                    f["h_rows"](l, CTX)
                    experts(engine, eng, l, CTX, mixing(l, LAT, f), f)
                else:
                    run(engine, mixing(l, LAT, f))
                f["h_rows"](l, LAT)
                experts(engine, eng, l, LAT, during_latent(l, f), f)

        block = ctx.enter_context(nc.Block())

        @block.sync
        def _(sp):
            for name, dst in (("cvec", cvec[:, 1, :, :]), ("x", None), ("ident", ident[:, :]), ("half_ones", half_ones[:, :]),
                              ("norm_cols", norm_cols[:, :]), ("dft", dft[:, :, :]), ("idft", idft[:, :, :]),
                              ("tab", tab[:, :, :]), ("cols", cols[:, :, :]), ("fw1", fw1[:, :, :]),
                              ("fw2", fw2[:, :, :]), ("fcol", fcol[:, :, :]), ("iota16", iota16[:, :])):
                if name == "x":
                    sp.dma_start(xT[:, :, 0:SEQ], dram["ctx"]).then_inc(*consts_in.mark())
                    sp.dma_start(xT[:, :, SEQ:2 * SEQ], dram["x"]).then_inc(*consts_in.mark("all"))
                else:
                    sp.dma_start(dst, dram[name]).then_inc(*consts_in.mark("all"))

            def load_layer(l):
                if l:
                    sp.wait_ge(*v_ready.at("expert", l - 1, LAT, TT - 1))
                sp.dma_start(rows[:, :], dram["rows"][l, :, :]).then_inc(*rows_in.mark(l))
                sp.dma_start(fdft, dram["fdft"]).then_inc(*filt_in.mark())
                sp.dma_start(decay, dram["decay"]).then_inc(*filt_in.mark())
                sp.dma_start(feat, dram["feat"]).then_inc(*filt_in.mark())
                sp.dma_start(fw3[:, :], dram["fw3"][l, :, :]).then_inc(*filt_in.mark(l))

            order = weight_order()
            for n, (kind, l, j, *s) in enumerate(order):
                if kind == "mod" and j == 0:
                    load_layer(l)
                if kind == "wq" and j == 2:
                    sp.wait_ge(*full.at("out", l, *s, D // CW - 1))
                    sp.dma_start(keys, dram["keys"][l, :, :, :]).then_inc(*keys_in.mark(l, *s))
                if n >= WS:
                    sp.wait_ge(*full.at(*product_of(*order[n - WS])))
                sp.dma_start(w_sb[:, n % WS, :, :], dram[kind][l, j, :, :, :]).then_inc(*weights_in[n % WS].mark(n))
            for c in range(KC):
                sp.wait_ge(*v_ready.at("x_ffn", DEPTH - 1, LAT, TT - 1, c))
                sp.dma_start(dram["y"][c * P:(c + 1) * P, :], xT[:, c, SEQ:2 * SEQ]).then_inc(*out_done.mark(c))
            sp.wait_ge(*out_done.at(KC - 1))

        @block.tensor
        def _(pe):
            mm = pe.matmul
            order = weight_order()
            used = [0]
            pe.sem_inc(v_used.sem, V_0)

            def take(*key):
                n = len(taken)
                if n >= BANKS:
                    pe.wait_ge(*emptied(taken[n - BANKS]))
                taken.append(key)
                return banks[n % BANKS]

            def weights(*what):
                n = used[0]
                assert order[n] == what, (order[n], what)
                used[0] += 1
                pe.wait_ge(*weights_in[n % WS].at(n))
                return w_sb[:, n % WS, :, :]

            def modulation(l):
                pe.wait_ge(*v_ready.at("silu"))
                pe.wait_ge(*consts_in.at("all"))

                def turn(n):
                    pe.wait_ge(*read_s.at("mod", l, n))
                    bank = take("modT", l, n)
                    for i in range(4):
                        ins = pe.transpose(bank[:, 2 * i:2 * i + 2], modrow[:, n % 2, i * P:(i + 1) * P], ident[0:2, 0:2])
                    ins.then_inc(*full.mark("modT", l, n))

                for n in range(12):
                    bank = take("mod", l, n)
                    for j in range(2):
                        w = weights("mod", l, 2 * n + j)
                        for k in range(KC):
                            ins = mm(bank[0:2, j * CW:(j + 1) * CW], cvec[:, 0, k, :], w[:, k, :],
                                     start=k == 0, stop=k == KC - 1)
                        ins.then_inc(*full.mark("mod" if j else "modhalf", l, n))
                    if n:
                        turn(n - 1)
                        yield "mod", n - 1
                turn(11)
                yield "mod", 11

            def filters(l):
                pe.wait_ge(*filt_in.at(l))
                bank = take("fh1", l)
                mm(bank[0:64, 0:SEQ], fw1[:, l, :], feat, start=True, stop=True).then_inc(*full.mark("fh1", l))
                pe.wait_ge(*s_ready.at("fh1", l))
                bank = take("fh2", l)
                mm(bank[0:64, 0:SEQ], fw2[:, l, :], fh[0:64, :], start=True, stop=True).then_inc(*full.mark("fh2", l))
                pe.wait_ge(*s_ready.at("fh2", l))
                for t in range(TT):
                    for h in range(2):
                        bank = take("filt", l, t, h)
                        mm(bank[:, :], fh[:, t * P:(t + 1) * P], fw3[:, h * 512:(h + 1) * 512],
                           start=True, stop=True).then_inc(*full.mark("filt", l, t, h))
                yield "filt"
                pe.wait_ge(*read_v.at("filt", l, TT - 1, 1))
                for b in range(NFB):
                    bank = take("spec", l, b)
                    n = 0
                    for d in range(2):
                        for t in range(TT):
                            ins = mm(bank[:, :], fdft[:, d * TT + t, b * P:(b + 1) * P], filt[:, t, d:4:2, :],
                                     start=n == 0, stop=n == 3)
                            n += 1
                    ins.then_inc(*full.mark("spec", l, b))
                    yield "spec", b
                pe.wait_ge(*s_ready.at("afilt", l))
                bank = take("fnorm", l)
                for o in range(2):
                    for c in range(2):
                        n = 0
                        for d in range(2):
                            for t in range(TT):
                                ins = mm(bank[:, 2 * o + c:2 * o + c + 1], afilt[:, t, 2 * o + d, c * P:(c + 1) * P],
                                         norm_cols[:, int(d == 1 and t == 0):int(d == 1 and t == 0) + 1],
                                         start=n == 0, stop=n == 3)
                                n += 1
                ins.then_inc(*full.mark("fnorm", l))
                yield "fnorm",

            def norm(which, l, s):
                pe.wait_ge(*v_ready.at("sq", which, l, s))
                bank = take("norm", which, l, s)
                for k in range(KC):
                    ins = mm(bank[:, 0:SEQ], ones[:, :], sq[:, k * SEQ:(k + 1) * SEQ], start=k == 0, stop=k == KC - 1)
                ins.then_inc(*full.mark("norm", which, l, s))
                yield "norm",

            def in_proj(l, s):
                pe.wait_ge(*s_ready.at("h", "mix", l, s))
                for j in range(N_IN) if is_full(l, s) else (DK, WGK, DV, WGV):
                    w = weights("in", l, j, s)
                    bank = take("in", l, s, j)
                    for i in range(2):
                        for k in range(KC):
                            if j < HY0:
                                ins = mm(bank[:, i * CW:(i + 1) * CW], hT[:, k, i * P:(i + 1) * P], w[:, k, :],
                                         start=k == 0, stop=k == KC - 1)
                            else:
                                ins = mm(bank[:, i * CW:(i + 1) * CW], w[:, k, i * P:(i + 1) * P], hT[:, k, :],
                                         start=k == 0, stop=k == KC - 1)
                    ins.then_inc(*full.mark("in", l, s, j))
                    yield "in", j

            def turn_qk(l, s):
                yield from wait_qk()
                pe.wait_ge(*v_step.at("qk", l, s))
                groups = (0, 1), (2, 3), (4, 5, 6, 7), (8, 9)
                for t in range(TT):
                    for g, blocks in enumerate(groups):
                        if not is_full(l, s) and g in (0, 2):
                            continue
                        bank = take("qkT", l, s, t, g)
                        for i, b in enumerate(blocks):
                            ins = pe.transpose(bank[:, i * P:(i + 1) * P], ptok[:, t, b * P:(b + 1) * P], ident[:, :])
                        ins.then_inc(*full.mark("qkT", l, s, t, g))
                    yield "qkT", t

            def attention(l, s):
                units = [(t, h) for t in range(TT) for h in range(12)]
                nk = SEQ if s == CTX else 2 * SEQ
                nb = nk // P
                pe.wait_ge(*read_s.at("qkT", l, s, TT - 1, 3))

                def scores(t, h):
                    for c in range(2 if h < 4 else 1):
                        bank = take("s", l, s, t, h, c)
                        if h < 4:
                            qb, kb, at, d = h // 2, h // 2, 64 * (h % 2) + 32 * c, 32
                        else:
                            qb, kb, at, d = 2 + 2 * (h // 4 - 1) + h % 2, 1 + h // 4, 64 * (h % 4 // 2), 64
                        mm(bank[:, 0:nk], qT[at:at + d, qb, t * P:(t + 1) * P], kT[at:at + d, kb, 0:nk],
                           start=True, stop=True).then_inc(*full.mark("s", l, s, t, h, c))

                def turn(t, h):
                    pe.wait_ge(*(v_ready.at("prob", l, s, t, h) if h < 4 else read_s.at("s", l, s, t, h, 0)))
                    bank = take("pT", l, s, t, h)
                    i = (t * 12 + h) % 2
                    for b in range(nb):
                        ins = pe.transpose(bank[:, b * P:(b + 1) * P], prob[:, i, 0, b * P:(b + 1) * P], ident[:, :])
                    ins.then_inc(*full.mark("pT", l, s, t, h))

                def values(t, h):
                    if h % 4 == 0 and (t, h) != (0, 0):
                        pe.wait_ge(*read_v.at("o", l, s, *units[t * 12 + h - 1]))
                    pe.wait_ge(*read_s.at("pT", l, s, t, h))
                    v = 64 * h if h < 4 else 256 + 128 * (h // 4 - 1) + 64 * (h % 4 // 2)
                    i = (t * 12 + h) % 2
                    for b in range(nb):
                        ins = mm(obank[:, 64 * (h % 4):64 * (h % 4) + 64], probT[:, i, b, :], vtok[:, b, v:v + 64],
                                 start=b == 0, stop=b == nb - 1)
                    ins.then_inc(*full.mark("o", l, s, t, h))

                n = len(units)
                for i in range(n + 2):
                    if i < n:
                        scores(*units[i])
                    if 1 <= i <= n:
                        turn(*units[i - 1])
                    if i >= 2:
                        values(*units[i - 2])
                    yield "unit", i

            def turn_o(l, s):
                pe.wait_ge(*v_ready.at("onorm", l, s))
                for t in range(TT):
                    for g in range(2):
                        bank = take("oT", l, s, t, g)
                        for i in range(3):
                            b = 3 * g + i
                            ins = pe.transpose(bank[:, i * P:(i + 1) * P], otok[:, t, b * P:(b + 1) * P], ident[:, :])
                        ins.then_inc(*full.mark("oT", l, s, t, g))
                yield "o",

            def hyena(l, s):
                yield "conv",
                for o in range(2):
                    pe.wait_ge(*v_ready.at("z", l, s, o))
                    bank = take("zt", l, s, o)
                    for t in range(TT):
                        for c in range(2):
                            src = uc[:, c, t * P:(t + 1) * P] if o == 0 else hy[:, c, t * P:(t + 1) * P]
                            ins = pe.transpose(bank[:, t * CW + c * P:t * CW + (c + 1) * P], src, ident[:, :])
                    ins.then_inc(*full.mark("zt", l, s, o))
                    pe.wait_ge(*read_s.at("zt", l, s, o))
                    for r in range(2):
                        bank = take("zf", l, s, o, r)
                        for b in range(2):
                            for t in range(TT):
                                ins = mm(bank[:, b * CW:(b + 1) * CW], dft[:, t, (2 * r + b) * P:(2 * r + b + 1) * P],
                                         zt[:, t, :], start=t == 0, stop=t == TT - 1)
                        ins.then_inc(*full.mark("zf", l, s, o, r))
                    yield "zf", o
                    pe.wait_ge(*v_ready.at("yspec", l, s, o))
                    bank = take("y", l, s, o)
                    for c in range(2):
                        for b in range(4):
                            ins = mm(bank[:, c * SEQ:(c + 1) * SEQ], yspec[:, b, c * P:(c + 1) * P], idft[:, b, :],
                                     start=b == 0, stop=b == 3)
                    ins.then_inc(*full.mark("y", l, s, o))
                    yield "y", o
                pe.wait_ge(*v_ready.at("hysq", l, s))
                bank = take("hynorm", l, s)
                for c in range(2):
                    ins = mm(bank[:, c * SEQ:(c + 1) * SEQ], half_ones[:, :], hy[:, 2 + c, :], start=True, stop=True)
                ins.then_inc(*full.mark("hynorm", l, s))
                yield "hynorm",

            def out_proj(l, s):
                pe.wait_ge(*read_s.at("oT", l, s, TT - 1, 1))
                pe.wait_ge(*v_ready.at("mixT", l, s))
                for j in range(D // CW):
                    w = weights("out", l, j, s)
                    bank = take("out", l, s, j)
                    for i in range(2):
                        for k in range(KC):
                            ins = mm(bank[:, i * SEQ:(i + 1) * SEQ], w[:, k, i * P:(i + 1) * P], mixT[:, k, :],
                                     start=k == 0, stop=k == KC - 1)
                    ins.then_inc(*full.mark("out", l, s, j))
                    yield "out", j

            def peer_queries(l, s):
                pe.wait_ge(*s_ready.at("h", "ffn", l, s))
                def key_scores(j):
                    pe.wait_ge(*read_s.at("pq", l, s, j))
                    bank = take("ks", l, s, j)
                    for t in range(TT):
                        for i in range(2):
                            ins = mm(bank[:, (2 * t + i) * P:(2 * t + i + 1) * P], pq[:, j % 2, i, t * P:(t + 1) * P],
                                     keys[:, 2 * j + i, :], start=True, stop=True)
                    ins.then_inc(*full.mark("ks", l, s, j))

                for j in range(HEADS):
                    w = weights("wq", l, j, s)
                    bank = take("pq", l, s, j)
                    for i in range(2):
                        for k in range(KC):
                            ins = mm(bank[:, i * SEQ:(i + 1) * SEQ], w[:, k, i * P:(i + 1) * P], hT[:, k, :],
                                     start=k == 0, stop=k == KC - 1)
                    ins.then_inc(*full.mark("pq", l, s, j))
                    if j == 0:
                        pe.wait_ge(*keys_in.at(l, s))
                    else:
                        key_scores(j - 1)
                    yield "pq", j
                key_scores(HEADS - 1)
                yield "pq", HEADS
                for t in range(TT):
                    yield "route", t

            def h_rows(l, s):
                for t in range(TT):
                    for g in range(2):
                        bank = take("h2", l, s, t, g)
                        for i in range(4):
                            ins = pe.transpose(bank[:, i * P:(i + 1) * P], hT[:, 4 * g + i, t * P:(t + 1) * P], ident[:, :])
                        ins.then_inc(*full.mark("h2", l, s, t, g))

            def expert_start(l, s, t):
                q = peer_tiles.index((l, s, t))
                if q:
                    pe.wait_ge(*s_ready.at("yacc", *peer_tiles[q - 1]))
                pe.wait_ge(*read_s.at("h2", l, s, TT - 1, 1))
                for a in range(2):
                    mm(acc[a][:, :], zeros[:, :], h2tok[:, t, 0:512], start=True, stop=False, skip_group_check=True)

            def expert_steps(l, s, t, i, n):
                for g in range(n):
                    for j in range(STEP):
                        pe.wait_ge(v_in[j].sem, i * 16 * n + (16 * g + 16))
                        pe.wait_ge(diag_ready.sem, i * STEP * n + (STEP * g + j + 1 + DIAG_0))
                        mm(acc[0][:, :], diag[:, j, :], vrow[:, j, 0:512], start=False, stop=False, skip_group_check=True)
                        mm(acc[1][:, :], diag[:, j, :], vrow[:, j, 512:D], start=False, stop=False,
                           skip_group_check=True).then_inc(v_used.sem, 1)

            def expert_end(l, s, t):
                for a in range(2):
                    ins = mm(acc[a][:, :], zeros[:, :], h2tok[:, t, 0:512], start=False, stop=True, skip_group_check=True)
                ins.then_inc(*full.mark("acc", l, s, t))
                turn_y(l, s, t)

            def turn_y(l, s, t):
                pe.wait_ge(*s_ready.at("yacc", l, s, t))
                for g in range(2):
                    bank = take("yT", l, s, t, g)
                    for i in range(4):
                        ins = pe.transpose(bank[:, i * P:(i + 1) * P], h2tok[:, t, (4 * g + i) * P:(4 * g + i + 1) * P], ident[:, :])
                    ins.then_inc(*full.mark("yT", l, s, t, g))

            whole("PE", pe, {"modulation": modulation, "filters": filters, "in_proj": in_proj, "turn_qk": turn_qk,
                       "attention": attention, "hyena": hyena, "out_proj": out_proj,
                       "peer_queries": peer_queries, "h_rows": h_rows, "turn_o": turn_o, "mix_norm": lambda l, s: norm("mix", l, s),
                       "ffn_norm": lambda l, s: norm("ffn", l, s),
                       "expert_start": expert_start, "expert_steps": expert_steps, "expert_end": expert_end})

        @block.scalar
        def _(act):
            ac = nc.scalar.activation

            def done(ins, sig=s_step, *event):
                ins.then_inc(*sig.mark(*event))
                act.wait_ge(sig.sem, sig.n)

            act.sem_inc(diag_ready.sem, DIAG_0)
            act.wait_ge(*consts_in.at("all"))
            done(ac(cvec[:, 2, :, :], cvec[:, 1, :, :], ACT.Exp, scale=-1.0), s_ready, "exp_c")

            def modulation(l):
                if l:
                    act.wait_ge(*v_ready.at("expert", l - 1, LAT, TT - 1))
                for n in range(12):
                    act.wait_ge(*full.at("mod", l, n))
                    if n >= 2:
                        act.wait_ge(*full.at("modT", l, n - 2))
                    bank = bank_of("mod", l, n)
                    done(ac(modrow[:, n % 2, :], bank[0:2, :], ACT.Copy), read_s, "mod", l, n)
                    if n:
                        yield "mod", n - 1
                yield "mod", 11

            def filters(l):
                act.wait_ge(*v_ready.at("lam", l))
                done(ac(lam[:, 66:68], lam[:, 64:66], ACT.Exp), s_ready, "lam", l)
                for n in (1, 2):
                    act.wait_ge(*v_ready.at(f"fr{n}", l))
                    done(ac(fh[0:64, :], fr, ACT.Sin), s_ready, f"fh{n}", l)
                yield "filt"
                act.wait_ge(*read_v.at("filt", l, TT - 1, 1))
                done(ac(afilt, filt, ACT.Abs), s_ready, "afilt", l)
                for b in range(NFB):
                    act.wait_ge(*full.at("spec", l, b))
                    done(ac(spec[:, b, :, :], bank_of("spec", l, b)[:, :].rearrange("p (o n) -> p o n", o=2), ACT.Copy),
                         read_s, "spec", l, b)
                    yield "spec", b
                yield "fnorm",

            def scaled(which, l, s):
                a, sh = (amix, 0) if which == "mix" else (affn, 24)
                act.wait_ge(*v_ready.at("xn", which, l, s))
                for k in range(KC):
                    ins = ac(hT[:, k, :], hT[:, k, :], ACT.Identity, bias=modT[:, l, sh + k, s:s + 1], scale=a[:, l, k, s:s + 1])
                    ins.then_inc(*(s_ready.mark("h", which, l, s) if k == KC - 1 else s_step.mark()))
                yield "norm",

            def in_proj(l, s):
                for j in range(N_IN) if is_full(l, s) else (DK, WGK, DV, WGV):
                    act.wait_ge(*full.at("in", l, s, j))
                    bank = bank_of("in", l, s, j)[:, :].rearrange("p (i n) -> p i n", i=2)
                    if j in QK_AT:
                        dst = ptok[:, :, QK_AT[j]:QK_AT[j] + CW]
                    elif j < HY0:
                        dst = vtok[:, 2 * s:2 * s + 2, (j - DV) * CW:(j - DV + 1) * CW]
                    else:
                        dst = upad[:, 2 * (j - HY0):2 * (j - HY0) + 2, 1:SEQ + 1]
                    done(ac(dst, bank, ACT.Copy), read_s, "in", l, s, j)
                    yield "in", j

            def turn_qk(l, s):
                yield from wait_qk()
                dests = (qT, 0), (kT, 0), (qT, 2), (kT, 2)
                for t in range(TT):
                    for g, (buf, at) in enumerate(dests):
                        if not is_full(l, s) and g in (0, 2):
                            continue
                        act.wait_ge(*full.at("qkT", l, s, t, g))
                        n = 4 if g == 2 else 2
                        off = t * P + (s * SEQ if buf is kT else 0)
                        bank = bank_of("qkT", l, s, t, g)[:, 0:n * P].rearrange("p (b n) -> p b n", b=n)
                        done(ac(buf[:, at:at + n, off:off + P], bank, ACT.Copy), read_s, "qkT", l, s, t, g)
                    yield "qkT", t

            def attention(l, s):
                units = [(t, h) for t in range(TT) for h in range(12)]
                nk = SEQ if s == CTX else 2 * SEQ
                nb = nk // P

                def exps(t, h):
                    i = (t * 12 + h) % 2
                    z = (t * 12 + h) % 8
                    scale = (32 if h < 4 else 64) ** -0.5
                    for c in range(2 if h < 4 else 1):
                        act.wait_ge(*v_ready.at("negm", l, s, t, h, c))
                        if t * 12 + h >= 2:
                            act.wait_ge(*full.at("pT", l, s, *units[t * 12 + h - 2]))
                        bank = bank_of("s", l, s, t, h, c)
                        done(ac(prob[:, i, c, 0:nk], bank[:, 0:nk], ACT.Exp, bias=negm[:, i, c:c + 1], scale=scale,
                                accum_out=zsum[:, z, c:c + 1]), read_s, "s", l, s, t, h, c)
                    if 4 <= h < 8:
                        done(ac(sinke[:, i:i + 1], negsink[:, h - 4:h - 3], ACT.Exp, bias=negm[:, i, 0:1], scale=-1.0),
                             s_ready, "sinke", l, s, t, h)

                def turned(t, h):
                    i = (t * 12 + h) % 2
                    act.wait_ge(*full.at("pT", l, s, t, h))
                    if t * 12 + h >= 2:
                        act.wait_ge(*full.at("o", l, s, *units[t * 12 + h - 2]))
                    bank = bank_of("pT", l, s, t, h)[:, 0:nk].rearrange("p (b n) -> p b n", b=nb)
                    done(ac(probT[:, i, 0:nb, :], bank, ACT.Copy), read_s, "pT", l, s, t, h)

                for i in range(len(units) + 1):
                    if i < len(units):
                        exps(*units[i])
                    if i:
                        turned(*units[i - 1])
                    yield "unit", i
                yield "unit", len(units) + 1

            def turn_o(l, s):
                for t in range(TT):
                    for g in range(2):
                        act.wait_ge(*full.at("oT", l, s, t, g))
                        for i in range(3):
                            b = 3 * g + i
                            done(ac(mixT[:, b, t * P:(t + 1) * P], bank_of("oT", l, s, t, g)[:, i * P:(i + 1) * P],
                                    ACT.Copy, scale=gout[:, b:b + 1]),
                                 *((read_s, "oT", l, s, t, g) if i == 2 else (s_step,)))
                yield "o",

            def hyena(l, s):
                yield "conv",
                for o in range(2):
                    act.wait_ge(*full.at("zt", l, s, o))
                    done(ac(zt[:, :, :], bank_of("zt", l, s, o)[:, :].rearrange("p (t n) -> p t n", t=TT), ACT.Copy),
                         read_s, "zt", l, s, o)
                    yield "zf", o
                    yield "y", o
                yield "hynorm",

            def out_proj(l, s):
                for j in range(D // CW):
                    yield "out", j

            def peer_queries(l, s):
                for j in range(HEADS):
                    act.wait_ge(*full.at("pq", l, s, j))
                    if j >= 2:
                        act.wait_ge(*full.at("ks", l, s, j - 2))
                    done(ac(pq[:, j % 2, :, :], bank_of("pq", l, s, j)[:, :].rearrange("p (i n) -> p i n", i=2),
                            ACT.Copy), read_s, "pq", l, s, j)
                    yield "pq", j
                yield "pq", HEADS
                for t in range(TT):
                    act.wait_ge(*v_ready.at("best", l, s, t))
                    done(ac(gate[:, s, t, :], gate[:, s, t, :], ACT.Exp), s_ready, "gate", l, s, t)
                    yield "route", t

            def h_rows(l, s):
                for t in range(TT):
                    for g in range(2):
                        act.wait_ge(*full.at("h2", l, s, t, g))
                        done(ac(h2tok[:, t, g * 512:(g + 1) * 512], bank_of("h2", l, s, t, g)[:, :], ACT.Copy),
                             read_s, "h2", l, s, t, g)

            def expert_start(l, s, t):
                pass

            def expert_steps(l, s, t, i, n):
                for g in range(n):
                    b = g if n == 2 else i % 2
                    act.wait_ge(poly_ready.sem, i * n + (g + 1))
                    ac(th[:, b, :], poly[:, b, :], ACT.Tanh, scale=GELU_S).then_inc(th_ready.sem, 1)
                    act.wait_ge(w_ready.sem, i * n + (g + 1))
                    for j in range(STEP):
                        act.wait_ge(v_used.sem, i * n * STEP + (STEP * (g - 1) + j + 1 + V_0))
                        ac(diag[:, j, :], ident[:, :], ACT.Copy, scale=wexp[:, b, j:j + 1]).then_inc(diag_ready.sem, 1)

            def expert_end(l, s, t):
                act.wait_ge(*full.at("acc", l, s, t))
                for a in range(2):
                    done(ac(h2tok[:, t, a * 512:(a + 1) * 512], acc[a][:, :], ACT.Copy),
                         *((s_ready, "yacc", l, s, t) if a else (s_step,)))

            whole("ACT", act, {"modulation": modulation, "filters": filters, "in_proj": in_proj, "turn_qk": turn_qk,
                       "attention": attention, "hyena": hyena, "out_proj": out_proj,
                       "peer_queries": peer_queries, "h_rows": h_rows, "turn_o": turn_o, "mix_norm": lambda l, s: scaled("mix", l, s),
                       "ffn_norm": lambda l, s: scaled("ffn", l, s),
                       "expert_start": expert_start, "expert_steps": expert_steps, "expert_end": expert_end})

        @block.vector
        def _(dve):
            v = nc.vector

            def done(ins, sig=v_step, *event):
                ins.then_inc(*sig.mark(*event))
                dve.wait_ge(sig.sem, sig.n)

            dve.sem_inc(u_used.sem, U_0)
            def root(x, n, y, t):
                done(v.tensor_scalar(x, x, EPS * n, None, ALU.add))
                done(v.tensor_scalar(y.bitcast(I32), x.bitcast(I32), -0.5, float(0x5F3759DF), ALU.mult, ALU.add))
                for k in range(3):
                    done(v.tensor_tensor(t, y, y, ALU.mult))
                    done(v.scalar_tensor_tensor(t, t, -0.5, x, ALU.mult, ALU.mult))
                    done(v.scalar_tensor_tensor(x if k == 2 else y, t, 1.5, y, ALU.add, ALU.mult))

            done(v.memset(ones[:, :], 1.0))
            done(v.memset(zeros[:, :], 0.0))
            done(v.memset(upad[:, :, :], 0.0))
            done(v.memset(sinke[:, :], 0.0))
            dve.wait_ge(*s_ready.at("exp_c"))
            done(v.tensor_scalar(cvec[:, 2, :, :], cvec[:, 2, :, :], 1.0, None, ALU.add))
            done(v.reciprocal(cvec[:, 2, :, :], cvec[:, 2, :, :]))
            done(v.tensor_tensor(cvec[:, 0, :, :], cvec[:, 1, :, :], cvec[:, 2, :, :], ALU.mult), v_ready, "silu")

            def modulation(l):
                for n in range(12):
                    dve.wait_ge(*full.at("modT", l, n))
                    bank = bank_of("modT", l, n)[:, 0:8].rearrange("p (c s) -> p c s", c=4)
                    b = cols[:, l, C_BMOD + 4 * n:C_BMOD + 4 * n + 4].unsqueeze(2).to_broadcast([P, 4, 2])
                    done(v.tensor_tensor(modT[:, l, 4 * n:4 * n + 4, :], bank, b, ALU.add), read_v, "modT", l, n)
                    yield "mod", n
                for a, at, g in ((amix, 8, C_GMIX), (affn, 32, C_GFFN)):
                    done(v.tensor_scalar(a[:, l, :, :], modT[:, l, at:at + 8, :], 1.0, math.sqrt(D), ALU.add, ALU.mult))
                    done(v.tensor_tensor(a[:, l, :, :], a[:, l, :, :], cols[:, l, g:g + 8].unsqueeze(2).to_broadcast([P, 8, 2]), ALU.mult))
                lam0 = 0.8 - 0.6 * math.exp(-0.3 * l)
                done(v.tensor_scalar(gout[:, 0:2], cols[:, l, C_GOUT:C_GOUT + 2], (1.0 - lam0) * math.sqrt(HD), None, ALU.mult))
                done(v.tensor_scalar(gout[:, 2:8], cols[:, l, C_GOUT + 2:C_GOUT + 8], math.sqrt(HD), None, ALU.mult))
                dve.wait_ge(*rows_in.at(l))
                lv = rows[:, R_LAM:R_LAM + 128].rearrange("p (a b d) -> p a b d", a=2, b=2)
                lp = lam[:, 0:64].rearrange("p (a d) -> p a d", a=2)
                done(v.tensor_tensor(lp, lv[:, :, 0, :], lv[:, :, 1, :], ALU.mult))
                done(v.tensor_reduce(lam[:, 64:66], lp, X, ALU.add), v_ready, "lam", l)
                dve.wait_ge(*s_ready.at("lam", l))
                done(v.tensor_tensor(neglam[:, :], lam[:, 67:68], lam[:, 66:67], ALU.subtract))
                done(v.tensor_scalar(neglam[:, :], neglam[:, :], -lam0, None, ALU.add))
                done(v.tensor_scalar(negsink[:, :], rows[:, R_SINK:R_SINK + 4], -1.0, None, ALU.mult))
                for a, b, d in ((0, 512, 32), (512, QK_W, 64)):
                    done(v.tensor_scalar(rows[:, a:b], rows[:, a:b], math.sqrt(d), None, ALU.mult))

            def filters(l):
                dve.wait_ge(*filt_in.at(l))
                done(v.memset(fh[64:65, :], 1.0))
                for n in (1, 2):
                    dve.wait_ge(*full.at(f"fh{n}", l))
                    done(v.tensor_scalar(fr, bank_of(f"fh{n}", l)[0:64, 0:SEQ], fcol[:, l, n - 1:n], fcol[:, l, 2:3],
                                         ALU.add, ALU.mult), read_v, f"fh{n}", l)
                    done(v.tensor_scalar(fn, fr, 1.0 / (2 * math.pi), MAGIC, ALU.mult, ALU.add))
                    done(v.tensor_scalar(fn, fn, MAGIC, None, ALU.subtract))
                    done(v.scalar_tensor_tensor(fr, fn, -6.28125, fr, ALU.mult, ALU.add))
                    done(v.scalar_tensor_tensor(fr, fn, -(2 * math.pi - 6.28125), fr, ALU.mult, ALU.add))
                    done(v.tensor_scalar(fr, fr, 3.1415925, -3.1415925, ALU.min, ALU.max), v_ready, f"fr{n}", l)
                for t in range(TT):
                    for h in range(2):
                        dve.wait_ge(*full.at("filt", l, t, h))
                        done(v.tensor_tensor(filt[:, t, 2 * h:2 * h + 2, :],
                                             bank_of("filt", l, t, h)[:, :].rearrange("p (o n) -> p o n", o=2),
                                             decay[:, t:t + 1, :].to_broadcast([P, 2, SEQ]), ALU.mult),
                             read_v, "filt", l, t, h)
                yield "filt"
                for b in range(NFB):
                    yield "spec", b
                dve.wait_ge(*full.at("fnorm", l))
                done(v.reciprocal(rnorm[:, :], bank_of("fnorm", l)[:, 0:4]), read_v, "fnorm", l)
                yield "fnorm",

            def norm(which, l, s):
                xs = xT[:, :, s * SEQ:(s + 1) * SEQ]
                sqv = sq.rearrange("p (k n) -> p k n", k=KC)
                if which == "mix":
                    dve.wait_ge(*read_s.at("spec", l, NFB - 1))
                else:
                    dve.wait_ge(*full.at("out", l, s, D // CW - 1))
                done(v.tensor_tensor(sqv, xs, xs, ALU.mult), v_ready, "sq", which, l, s)
                dve.wait_ge(*full.at("norm", which, l, s))
                done(v.tensor_copy(rstd[:, :], bank_of("norm", which, l, s)[:, 0:SEQ]), read_v, "norm", which, l, s)
                root(rstd[:, :], D, sq[:, 0:SEQ], sq[:, SEQ:2 * SEQ])
                done(v.tensor_tensor(hT[:, :, :], xs, rstd[:, :].unsqueeze(1).to_broadcast([P, KC, SEQ]), ALU.mult),
                     v_ready, "xn", which, l, s)
                yield "norm",

            def groups(l, s):
                return ((0, 512, 32), (512, QK_W, 64)) if is_full(l, s) else ((256, 512, 32), (1024, QK_W, 64))

            def qk(l, s):
                dve.wait_ge(*read_s.at("in", l, s, WGK))
                for r, (a, b, d) in enumerate(groups(l, s)):
                    n = (b - a) // d
                    for t in range(TT):
                        x = ptok[:, t, a:b]
                        x4, q4, r4 = (z.rearrange("p (h d) -> p h d", d=d) for z in (x, qk_a[:, a:b], qk_b[:, a:b]))
                        st = stat[:, 0:n]
                        done(v.tensor_tensor(qk_a[:, a:b], x, x, ALU.mult))
                        done(v.tensor_reduce(st, q4, X, ALU.add))
                        root(st, d, qk_b[:, 0:n], qk_b[:, n:2 * n])
                        done(v.tensor_tensor(x4, x4, st.unsqueeze(2).to_broadcast([P, n, d]), ALU.mult))
                        done(v.tensor_tensor(x, x, rows[:, a:b], ALU.mult))
                        if s == CTX:
                            yield "qk", r, t
                            continue
                        h = d // 2
                        tc, ts = (T_C32, T_S32) if d == 32 else (T_C64, T_S64)
                        cos = tab[:, t, tc:tc + h].unsqueeze(1).to_broadcast([P, n, h])
                        sin = tab[:, t, ts:ts + h].unsqueeze(1).to_broadcast([P, n, h])
                        lo, hi = slice(0, h), slice(h, d)
                        done(v.tensor_tensor(q4[:, :, lo], x4[:, :, lo], cos, ALU.mult))
                        done(v.tensor_tensor(q4[:, :, hi], x4[:, :, hi], cos, ALU.mult))
                        done(v.tensor_tensor(r4[:, :, lo], x4[:, :, hi], sin, ALU.mult))
                        done(v.tensor_tensor(r4[:, :, hi], x4[:, :, lo], sin, ALU.mult))
                        done(v.tensor_tensor(x4[:, :, lo], q4[:, :, lo], r4[:, :, lo], ALU.subtract))
                        done(v.tensor_tensor(x4[:, :, hi], q4[:, :, hi], r4[:, :, hi], ALU.add))
                        yield "qk", r, t
                v_step.also("qk", l, s)

            def turn_qk(l, s):
                for t in range(TT):
                    yield "qkT", t

            def in_proj(l, s):
                for j in range(N_IN) if is_full(l, s) else (DK, WGK, DV, WGV):
                    yield "in", j

            def attention(l, s):
                units = [(t, h) for t in range(TT) for h in range(12)]
                nk = SEQ if s == CTX else 2 * SEQ

                def probs(t, h):
                    return s_ready.at("sinke", l, s, t, h) if 4 <= h < 8 else read_s.at("s", l, s, t, h, int(h < 4))

                def maxima(t, h):
                    i = (t * 12 + h) % 2
                    scale = (32 if h < 4 else 64) ** -0.5
                    for c in range(2 if h < 4 else 1):
                        dve.wait_ge(*full.at("s", l, s, t, h, c))
                        bank = bank_of("s", l, s, t, h, c)
                        if 4 <= h < 8 and s == LAT:
                            far = bank[:, SEQ + (1 - t) * P:SEQ + (2 - t) * P]
                            m = tab[:, t, T_MASK:T_MASK + P]
                            done(v.tensor_tensor(far, far, m, ALU.add))
                        done(v.tensor_reduce(mx[:, i, c:c + 1], bank[:, 0:nk], X, ALU.max))
                        if 4 <= h < 8:
                            done(v.tensor_scalar(negm[:, i, c:c + 1], mx[:, i, c:c + 1], -scale, negsink[:, h - 4:h - 3],
                                                 ALU.mult, ALU.min), v_ready, "negm", l, s, t, h, c)
                        else:
                            done(v.tensor_scalar(negm[:, i, c:c + 1], mx[:, i, c:c + 1], -scale, None,
                                                 ALU.mult), v_ready, "negm", l, s, t, h, c)

                def sums(t, h):
                    i, z = (t * 12 + h) % 2, (t * 12 + h) % 8
                    dve.wait_ge(*probs(t, h))
                    if 4 <= h < 8:
                        done(v.tensor_tensor(zsum[:, z, 0:1], zsum[:, z, 0:1], sinke[:, i:i + 1], ALU.add))
                    n = 2 if h < 4 else 1
                    done(v.reciprocal(rz[:, z, 0:n], zsum[:, z, 0:n]))
                    if h < 4:
                        done(v.tensor_tensor(rz[:, z, 1:2], rz[:, z, 1:2], neglam[:, :], ALU.mult))
                        done(v.tensor_scalar(prob[:, i, 0, 0:nk], prob[:, i, 0, 0:nk], rz[:, z, 0:1], None, ALU.mult))
                        done(v.scalar_tensor_tensor(prob[:, i, 0, 0:nk], prob[:, i, 1, 0:nk], rz[:, z, 1:2],
                                                    prob[:, i, 0, 0:nk], ALU.mult, ALU.add), v_ready, "prob", l, s, t, h)

                def outputs(t, h):
                    if h % 4 < 3:
                        return
                    z = (t * 12 + h - 3) % 8
                    dve.wait_ge(*full.at("o", l, s, t, h))
                    src = obank[:, 0:4 * HD].rearrange("p (h d) -> p h d", d=HD)
                    dst = otok[:, t, HD * (h - 3):HD * (h + 1)].rearrange("p (h d) -> p h d", d=HD)
                    if h < 4:
                        done(v.tensor_copy(dst, src), read_v, "o", l, s, t, h)
                    else:
                        done(v.tensor_tensor(dst, src, rz[:, z:z + 4, 0:1].to_broadcast([P, 4, HD]), ALU.mult),
                             read_v, "o", l, s, t, h)

                n = len(units)
                for i in range(n + 2):
                    if i < n:
                        if i >= 2:
                            dve.wait_ge(*probs(*units[i - 2]))
                        maxima(*units[i])
                    if 1 <= i <= n:
                        sums(*units[i - 1])
                    if i >= 2:
                        outputs(*units[i - 2])
                    yield "unit", i
                o4 = otok[:, :, :].rearrange("p t (h d) -> p t h d", d=HD)
                st = stat[:, 0:24].rearrange("p (t n) -> p t n", t=TT)
                done(v.tensor_tensor(osq, o4, o4, ALU.mult))
                done(v.tensor_reduce(st, osq, X, ALU.add))
                root(stat[:, 0:24], HD, qk_a[:, 0:24], qk_a[:, 24:48])
                done(v.tensor_tensor(o4, o4, st.unsqueeze(3).to_broadcast([P, TT, 12, HD]), ALU.mult), v_ready, "onorm", l, s)
                yield "o",

            def hyena(l, s):
                dve.wait_ge(*read_s.at("in", l, s, N_IN - 1))
                for c in range(6):
                    w = [cols[:, l, C_CONVW + 6 * i + c:C_CONVW + 6 * i + c + 1] for i in range(3)]
                    b = cols[:, l, C_CONVB + c:C_CONVB + c + 1]
                    done(v.tensor_scalar(uc[:, c, :], upad[:, c, 1:SEQ + 1], w[1], b, ALU.mult, ALU.add))
                    done(v.scalar_tensor_tensor(uc[:, c, :], upad[:, c, 0:SEQ], w[0], uc[:, c, :], ALU.mult, ALU.add))
                    done(v.scalar_tensor_tensor(uc[:, c, :], upad[:, c, 2:SEQ + 2], w[2], uc[:, c, :], ALU.mult, ALU.add),
                         *((v_ready, "z", l, s, 0) if c == 5 else (v_step,)))
                yield "conv",
                for o in range(2):
                    yield "zf", o
                    dve.wait_ge(*full.at("zf", l, s, o, 0))
                    dve.wait_ge(*full.at("zf", l, s, o, 1))
                    re, im = (bank_of("zf", l, s, o, r)[:, :].rearrange("p (b n) -> p b n", b=2) for r in range(2))
                    t1, t2 = hy[:, 4:6, :], hy[:, 6:8, :]
                    done(v.tensor_tensor(t1, re, spec[:, 0:2, o, :], ALU.mult))
                    done(v.tensor_tensor(t2, im, spec[:, 2:4, o, :], ALU.mult))
                    done(v.tensor_tensor(yspec[:, 0:2, :], t1, t2, ALU.subtract))
                    done(v.tensor_tensor(t1, re, spec[:, 2:4, o, :], ALU.mult), read_v, "zf", l, s, o, 0)
                    done(v.tensor_tensor(t2[:, 0:1, :], im[:, 0:1, :], spec[:, 4:5, o, :], ALU.mult))
                    done(v.tensor_tensor(t2[:, 1:2, :], im[:, 1:2, :], spec[:, 1:2, o, :], ALU.mult), read_v, "zf", l, s, o, 1)
                    done(v.tensor_tensor(yspec[:, 2:4, :], t1, t2, ALU.add), v_ready, "yspec", l, s, o)
                    dve.wait_ge(*full.at("y", l, s, o))
                    y = bank_of("y", l, s, o)[:, :].rearrange("p (c n) -> p c n", c=2)
                    for c in range(2):
                        z = uc[:, c, :] if o == 0 else hy[:, c, :]
                        hb = cols[:, l, C_HYB + 2 * o + c:C_HYB + 2 * o + c + 1]
                        done(v.tensor_scalar(z, z, hb, None, ALU.mult))
                        done(v.scalar_tensor_tensor(z, y[:, c, :], rnorm[:, 2 * o + c:2 * o + c + 1], z, ALU.mult, ALU.add),
                             *((read_v, "y", l, s, o) if c == 1 else (v_step,)))
                        done(v.tensor_tensor(hy[:, c, :], z, uc[:, 2 + 2 * o + c, :], ALU.mult),
                             *((v_ready, "z", l, s, 1) if c == 1 and o == 0 else (v_step,)))
                    yield "y", o
                done(v.tensor_tensor(hy[:, 2:4, :], hy[:, 0:2, :], hy[:, 0:2, :], ALU.mult), v_ready, "hysq", l, s)
                dve.wait_ge(*full.at("hynorm", l, s))
                bank = bank_of("hynorm", l, s)[:, :].rearrange("p (c n) -> p c n", c=2)
                done(v.tensor_copy(hy[:, 4:6, :], bank), read_v, "hynorm", l, s)
                root(hy[:, 4:6, :], HD, hy[:, 6:8, :], hy[:, 2:4, :])
                for c in range(2):
                    done(v.scalar_tensor_tensor(mixT[:, 6 + c, :], hy[:, c, :], gout[:, 6 + c:7 + c], hy[:, 4 + c, :],
                                                ALU.mult, ALU.mult),
                         *((v_ready, "mixT", l, s) if c else (v_step,)))
                yield "hynorm",

            def out_proj(l, s):
                for j in range(D // CW):
                    dve.wait_ge(*full.at("out", l, s, j))
                    for i in range(2):
                        c = 2 * j + i
                        xs = xT[:, c, s * SEQ:(s + 1) * SEQ]
                        done(v.scalar_tensor_tensor(xs, bank_of("out", l, s, j)[:, i * SEQ:(i + 1) * SEQ],
                                                    modT[:, l, 16 + c, s:s + 1], xs, ALU.mult, ALU.add),
                             *((read_v, "out", l, s, j) if i else (v_step,)))
                    yield "out", j

            def top16(src, tmp, vals, ids):
                done(v.max(vals[:, 0:8], src))
                done(v.max_index(ids[:, 0:8], vals[:, 0:8], src))
                done(v.match_replace(tmp, vals[:, 0:8], src, -3.0e38))
                done(v.max(vals[:, 8:16], tmp))

            def candidates(l, s, h):
                dve.wait_ge(*full.at("ks", l, s, h))
                bank = bank_of("ks", l, s, h)
                for t in range(TT):
                    for half in range(2):
                        i = 2 * t + half
                        ids = idx_a[:, t, half, h, :]
                        top16(bank[:, i * P:(i + 1) * P], work, top8[:, i, :], ids)
                        done(v.max_index(ids[:, 8:16], top8[:, i, 8:16], work),
                             *((read_v, "ks", l, s, h) if i == 3 else (v_step,)))
                    c3 = cand.rearrange("p (a b) -> p a b", a=TOPK)
                    done(v.tensor_tensor(c3, top8[:, 2 * t, :].unsqueeze(2).to_broadcast([P, TOPK, TOPK]),
                                         top8[:, 2 * t + 1, :].unsqueeze(1).to_broadcast([P, TOPK, TOPK]), ALU.add))
                    top16(cand, cand2, best[:, t, h, :], pos[:, t, h, :])
                    done(v.max_index(pos[:, t, h, 8:16], best[:, t, h, 8:16], cand2))

            def route(l, s, t):
                g3 = gate[:, s, t, :].rearrange("p (h k) -> p h k", h=HEADS)
                bt = best[:, t, :, :]
                done(v.tensor_tensor(g3, bt, bt[:, :, 0:1].to_broadcast([P, HEADS, TOPK]), ALU.subtract),
                     v_ready, "best", l, s, t)
                pv = pos[:, t, :, :].rearrange("p h k -> p (h k)")
                done(v.tensor_scalar(pij[:, 0, :], pv, 4, None, ALU.logical_shift_right))
                done(v.tensor_scalar(pij[:, 1, :], pv, 15, None, ALU.bitwise_and))
                done(v.tensor_copy(pijf[:, :, :], pij[:, :, :]))
                done(v.tensor_copy(idx_f[:, :, :, :], idx_a[:, t, :, :, :]))
                hot3 = hot.rearrange("p (e i) -> p e i", i=TOPK)
                hot4 = hot.rearrange("p (h k i) -> p h k i", h=HEADS, i=TOPK)
                for a in range(2):
                    done(v.tensor_tensor(hot3, pijf[:, a, :].unsqueeze(2).to_broadcast([P, NE, TOPK]),
                                         iota16[:, :].unsqueeze(1).to_broadcast([P, NE, TOPK]), ALU.is_equal))
                    done(v.tensor_tensor(hot4, hot4, idx_f[:, a, :, :].unsqueeze(2).to_broadcast([P, HEADS, TOPK, TOPK]), ALU.mult))
                    done(v.tensor_reduce(eij[:, a, :], hot3, X, ALU.add))
                done(v.scalar_tensor_tensor(eij[:, 0, :], eij[:, 0, :], float(N_KEYS), eij[:, 1, :], ALU.mult, ALU.add))
                if l:
                    done(v.tensor_scalar(eij[:, 0, :], eij[:, 0, :], float(l * N_EXPERTS), None, ALU.add))
                done(v.tensor_copy(expert[:, s, t, :], eij[:, 0, :]), v_ready, "expert", l, s, t)
                dve.wait_ge(*s_ready.at("gate", l, s, t))
                done(v.tensor_reduce(gz[:, 0, :], g3, X, ALU.add))
                done(v.reciprocal(gz[:, 1, :], gz[:, 0, :]))
                done(v.tensor_scalar(gz[:, 1, :], gz[:, 1, :], 0.5, None, ALU.mult))
                done(v.tensor_tensor(g3, g3, gz[:, 1, :].unsqueeze(2).to_broadcast([P, HEADS, TOPK]), ALU.mult))

            def peer_queries(l, s):
                yield "pq", 0
                for h in range(HEADS):
                    candidates(l, s, h)
                    yield "pq", h + 1
                for t in range(TT):
                    route(l, s, t)
                    yield "route", t

            def expert_start(l, s, t):
                if t == 0:
                    dve.wait_ge(*read_s.at("h2", l, s, TT - 1, 1))

            def expert_steps(l, s, t, i, n):
                q = peer_tiles.index((l, s, t))
                for g in range(n):
                    b = g if n == 2 else i % 2
                    x, pol, w = dots[:, b, :], poly[:, b, :], wexp[:, b, :]
                    for j in range(STEP):
                        dve.wait_ge(u_in[j].sem, i * 16 * n + (16 * g + 16))
                        v.tensor_tensor_reduce(urow[:, j, :], urow[:, j, :], h2tok[:, t, :], 1.0, 0.0,
                                               ALU.mult, ALU.add, x[:, j:j + 1]).then_inc(u_used.sem, 1)
                    dve.wait_ge(u_used.sem, i * n * STEP + (STEP * (g + 1) + U_0))
                    v.tensor_tensor(pol, x, x, ALU.mult).then_inc(gelu_step.sem, 1)
                    dve.wait_ge(gelu_step.sem, i * 3 * n + (3 * g + 1))
                    v.tensor_scalar(pol, pol, GELU_C, 1.0, ALU.mult, ALU.add).then_inc(gelu_step.sem, 1)
                    dve.wait_ge(gelu_step.sem, i * 3 * n + (3 * g + 2))
                    v.tensor_tensor(pol, pol, x, ALU.mult).then_inc(poly_ready.sem, 1)
                    dve.wait_ge(th_ready.sem, i * n + (g + 1))
                    v.scalar_tensor_tensor(th[:, b, :], th[:, b, :], 1.0, x, ALU.add, ALU.mult).then_inc(gelu_step.sem, 1)
                    dve.wait_ge(gelu_step.sem, i * 3 * n + (3 * g + 3))
                    dve.wait_ge(diag_ready.sem, i * n * STEP + (STEP * (g - 1) + DIAG_0))
                    at = i * n * STEP + (STEP * g - q * NE)
                    at = slice(at, at + STEP) if n == 1 else bass.ds(at, STEP)
                    v.tensor_tensor(w, th[:, b, :], gate[:, s, t, at], ALU.mult).then_inc(w_ready.sem, 1)
                    dve.wait_ge(w_ready.sem, i * n + (g + 1))

            def expert_end(l, s, t):
                add_experts(l, s, t)

            def add_experts(l, s, t):
                for g in range(2):
                    dve.wait_ge(*full.at("yT", l, s, t, g))
                    for i in range(4):
                        c = 4 * g + i
                        xs = xT[:, c, s * SEQ + t * P:s * SEQ + (t + 1) * P]
                        done(v.scalar_tensor_tensor(xs, bank_of("yT", l, s, t, g)[:, i * P:(i + 1) * P],
                                                    modT[:, l, 40 + c, s:s + 1], xs, ALU.mult, ALU.add),
                             v_ready, "x_ffn", l, s, t, c)
                    v_ready.also("yT", l, s, t, g)

            whole("DVE", dve, {"modulation": modulation, "filters": filters, "in_proj": in_proj, "turn_qk": turn_qk,
                       "attention": attention, "hyena": hyena, "out_proj": out_proj,
                       "peer_queries": peer_queries, "h_rows": lambda l, s: None, "qk": qk, "mix_norm": lambda l, s: norm("mix", l, s),
                       "ffn_norm": lambda l, s: norm("ffn", l, s),
                       "expert_start": expert_start, "expert_steps": expert_steps, "expert_end": expert_end})

        @block.gpsimd
        def _(pool):
            for q, (l, s, t) in enumerate(peer_tiles):
                ready = v_ready.at("expert", l, s, t)

                def u_step(i, b):
                    pool.wait_ge(v_used.sem, i * STEP + (V_0 - IXB * STEP + STEP))
                    pool.wait_ge(*ready)
                    nc.gpsimd.tensor_copy(ix[:, b, :], expert[:, s, t, bass.ds(i * STEP + (-q * NE), STEP)]).then_inc(ix_ready.sem, 1)
                    pool.wait_ge(ix_ready.sem, i + 1)
                    pool.sem_inc(row_free.sem, 1)
                    for j in range(STEP):
                        pool.wait_ge(u_used.sem, i * STEP + (j + 1 - STEP + U_0))
                        pool.sem_inc(row_free.sem, 1)
                        pool.indirect_dma_start(urow[:, j, :], None, dram["u"],
                                                bass.IndirectOffsetOnAxis(ap=ix[:, b, j:j + 1], axis=0)).then_inc(u_in[j].sem, 16)

                def v_step_(i, b):
                    for j in range(STEP):
                        pool.wait_ge(v_used.sem, i * STEP + (j + 1 - STEP + V_0))
                        pool.sem_inc(row_free.sem, 1)
                        pool.indirect_dma_start(vrow[:, j, :], None, dram["v"],
                                                bass.IndirectOffsetOnAxis(ap=ix[:, b, j:j + 1], axis=0)).then_inc(v_in[j].sem, 16)

                at = q * STEPS
                u_step(at, 0)
                with pool.Fori(at, at + STEPS - IXB, IXB) as i:
                    for b in range(IXB):
                        u_step(i + (b + 1), (b + 1) % IXB)
                        v_step_(i + b, b)
                for b in range(IXB):
                    if b < IXB - 1:
                        u_step(at + STEPS - IXB + b + 1, b + 1)
                    v_step_(at + STEPS - IXB + b, b)

        assert labels["PE"] == labels["ACT"] == labels["DVE"]
        ledger["bank_order"] = list(taken)


def constants():
    n = np.arange(SEQ, dtype=np.float64)
    f = np.arange(SEQ, dtype=np.float64)
    w = 2 * np.pi / 512
    re = np.cos(w * np.outer(n, f))
    im = -np.sin(w * np.outer(n, f))
    nyq = np.cos(np.pi * n)
    im_packed = im.copy()
    im_packed[:, 0] = nyq
    dft = np.concatenate([re, im_packed], 1)
    ire = np.cos(w * np.outer(f, n)) * 2 / 512
    ire[0] /= 2
    iim = -np.sin(w * np.outer(f, n)) * 2 / 512
    iim[0] = nyq / 512
    idft = np.concatenate([ire, iim], 0)
    def fil(sign):
        r, i = re.copy(), sign * im
        last = r[:, 0:P].copy()
        last[:, 0] = nyq
        m = np.concatenate([r, i, last], 1)
        if sign < 0:
            m[0] = 0
        return m
    fdft = np.concatenate([fil(1.0), fil(-1.0)], 0)
    t = np.linspace(0.0, 1.0, SEQ, dtype=np.float32)[:, None]
    wn = (np.float32(2.0 * math.pi / SEQ) * np.arange(SEQ, dtype=np.float32))[:, None]
    fb = np.linspace(1e-4, BANDS - 1, BANDS, dtype=np.float32)[None, :]
    ang = (fb * wn).astype(np.float64)
    feat = np.concatenate([t, np.cos(ang), -np.sin(ang)], -1)
    deltas = np.abs(np.linspace(math.log(1e-2) / 1.5, math.log(1e-2) / 0.3, SEQ))
    decay = np.exp(-t.astype(np.float64) * deltas)

    def rope(dim):
        pos = np.arange(SEQ)
        axis = dim // 2
        inv = 10000.0 ** (-np.arange(0, axis, 2) / axis)
        a = np.concatenate([(pos // GRID_W)[:, None] * inv, (pos % GRID_W)[:, None] * inv], -1)
        return np.cos(a), np.sin(a)

    (c32, s32), (c64, s64) = rope(32), rope(64)
    q, k = np.arange(P)[:, None], np.arange(P)[None, :]
    mask = np.concatenate([np.where(k <= q, 0.0, -1e30), np.where(k >= q, 0.0, -1e30)], 0)
    tab = np.concatenate([c32, s32, c64, s64, mask], 1)

    def tiles(a):
        return np.ascontiguousarray(a.reshape(-1, P, a.shape[-1]).transpose(1, 0, 2), np.float32)

    half = np.kron(np.eye(2), np.ones((HD, HD)))
    nc_ = np.ones((P, 2))
    nc_[0, 1] = 0
    return {
        "ident": np.eye(P, dtype=np.float32), "half_ones": half.astype(np.float32), "norm_cols": nc_.astype(np.float32),
        "dft": tiles(dft), "idft": tiles(idft), "fdft": tiles(fdft), "decay": tiles(decay),
        "feat": np.ascontiguousarray(feat.T, np.float32), "tab": tiles(tab),
        "iota16": np.ascontiguousarray(np.broadcast_to(np.arange(TOPK, dtype=np.float32), (P, TOPK))),
    }


def layouts(a):
    def chunks(w):
        L, _, n = w.shape
        return np.ascontiguousarray(w.reshape(L, KC, P, n // CW, CW).transpose(0, 3, 2, 1, 4))

    def col(v, n):
        return np.asarray(v).reshape(DEPTH, n, P).transpose(0, 2, 1)

    w = np.asarray(a["w_in"])
    pair = [0, 2, 1, 3]

    def heads(at):
        return [w[:, :, at + h * HD:at + (h + 1) * HD] for h in pair]

    w_in = np.concatenate([w[:, :, 0:256], *heads(768), *heads(1280), w[:, :, 256:512], w[:, :, 1024:1152],
                           w[:, :, 1536:1664], w[:, :, 512:768], w[:, :, 1152:1280], w[:, :, 1664:1792],
                           w[:, :, 1792:2560]], 2)
    cols = np.concatenate([
        col(a["b_mod"], 48), col(a["g_norm_mix"], 8), col(a["g_norm_ffn"], 8), col(a["g_mix_out"], 8),
        col(a["hy_conv_w"], 18), col(a["hy_conv_b"], 6), col(a["hy_bias"], 4)], 2)
    gd, gw, gg = (np.asarray(a[k]) for k in ("g_qk_diff", "g_qk_win", "g_qk_glob"))
    row = np.concatenate([
        np.tile(gd[:, 0], (1, 8)), np.tile(gd[:, 1], (1, 8)), np.tile(gw[:, 0], (1, 4)), np.tile(gg[:, 0], (1, 4)),
        np.tile(gw[:, 1], (1, 2)), np.tile(gg[:, 1], (1, 2)), a["sink_win"], np.asarray(a["lambda_diff"]).reshape(DEPTH, 128)], 1)
    rows = np.ascontiguousarray(np.broadcast_to(row[:, None, :], (DEPTH, P, N_ROWS)))
    cv = np.stack([a["c_ctx"], a["c"][0]], 1).reshape(KC, P, 2).transpose(1, 0, 2)
    keys = np.asarray(a["peer_keys"]).transpose(0, 4, 1, 2, 3).reshape(DEPTH, P, 16, P)
    return {
        "x": a["x"][0].T.reshape(KC, P, SEQ).transpose(1, 0, 2),
        "ctx": a["ctx"][0].T.reshape(KC, P, SEQ).transpose(1, 0, 2),
        "cvec": cv, "cols": cols.transpose(1, 0, 2), "rows": rows,
        "mod": chunks(np.asarray(a["w_mod"])), "in": chunks(w_in), "out": chunks(np.asarray(a["w_out"])),
        "wq": chunks(np.asarray(a["peer_wq"])), "keys": keys,
        "fw1": np.asarray(a["hy_w1"]).transpose(1, 0, 2), "fw2": np.asarray(a["hy_w2"]).transpose(1, 0, 2),
        "fw3": np.concatenate([a["hy_w3"], np.asarray(a["hy_b3"])[:, None, :]], 1),
        "fcol": np.stack([a["hy_b1"], a["hy_b2"], a["hy_freq"]], 2).transpose(1, 0, 2),
        "u": np.asarray(a["peer_u"]).reshape(DEPTH * N_EXPERTS, D), "v": np.asarray(a["peer_v"]).reshape(DEPTH * N_EXPERTS, D),
    }


def kernel(**inputs):
    import concourse.bacc as bacc
    from concourse.bass_utils import run_bass_kernel_spmd

    arrays = {n: np.asarray(v) for n, v in inputs.items()}
    arrays = {n: np.ascontiguousarray(v) for n, v in {**constants(), **layouts(arrays)}.items()}
    ledger = {}
    for _ in range(2):
        nc = bacc.Bacc("TRN2", target_bir_lowering=False, num_devices=1)
        dram = {n: nc.dram_tensor(f"in_{n}_dram", v.shape, F32, kind="ExternalInput").ap() for n, v in arrays.items()}
        dram["y"] = nc.dram_tensor("out_0_dram", (D, SEQ), F32, kind="ExternalOutput").ap()
        build(nc, dram, ledger)
    r = run_bass_kernel_spmd(nc, [{f"in_{n}_dram": v for n, v in arrays.items()}], core_ids=[0])
    return np.ascontiguousarray(r.results[0]["out_0_dram"].T)[None]
```
